# Optimizing a Trainium2 kernel written in Bass

```python
import jax, jax.numpy as jnp
from jax import lax
import numpy as np

D_MODEL = 1024
BATCH = 1
SEQ = 512
DEPTH = 1

LRU_WIDTH = D_MODEL // 2
LRU_HEADS = 8
LRU_HEAD_DIM = LRU_WIDTH // LRU_HEADS
CONV_WIDTH = 4
LRU_C = 8.0
POOL_WIDTH = D_MODEL // 2
POOL_WINDOWS = (2, 4, 8, 16)
POOL_GROUPS = len(POOL_WINDOWS)
POOL_GROUP_DIM = POOL_WIDTH // POOL_GROUPS
MIX_WIDTH = LRU_WIDTH + POOL_WIDTH
IN_WIDTH = 2 * LRU_WIDTH + POOL_WIDTH
N_EXPERTS = 32
TOP_K = 4
D_EXPERT = D_MODEL
SWIGLU_LIMIT = 7.0
SWIGLU_ALPHA = 1.702
EXPERT_BLOCK = 256
NORM_EPS = 1e-6

kernel_name = "hybrid_rglru_pool_moe_adaln"

def rms_norm(x, g):
    x32 = x.astype(jnp.float32)
    y = x32 * lax.rsqrt(jnp.mean(x32 * x32, axis=-1, keepdims=True) + NORM_EPS)
    return (y * g.astype(jnp.float32)).astype(x.dtype)

def modulate(h, shift, scale):
    return h * (1.0 + scale[:, None, :]) + shift[:, None, :]

def causal_depthwise_conv(x, w, b):
    S = x.shape[1]
    xp = jnp.pad(x, ((0, 0), (CONV_WIDTH - 1, 0), (0, 0)))
    y = b
    for k in range(CONV_WIDTH):
        s0 = CONV_WIDTH - 1 - k
        y = y + xp[:, s0:s0 + S] * w[k]
    return y

def _lin_combine(e1, e2):
    a1, b1 = e1
    a2, b2 = e2
    return a1 * a2, a2 * b1 + b2

def rg_lru(x, gate_a_w, gate_a_b, gate_x_w, gate_x_b, lam):
    B, S, _ = x.shape
    xh = x.reshape(B, S, LRU_HEADS, LRU_HEAD_DIM)
    r = jax.nn.sigmoid(jnp.einsum('bshi,hij->bshj', xh, gate_a_w).reshape(B, S, LRU_WIDTH) + gate_a_b)
    i = jax.nn.sigmoid(jnp.einsum('bshi,hij->bshj', xh, gate_x_w).reshape(B, S, LRU_WIDTH) + gate_x_b)
    log_a = -LRU_C * r.astype(jnp.float32) * jax.nn.softplus(-lam.astype(jnp.float32))
    a = jnp.exp(log_a)
    mult = jnp.sqrt(-jnp.expm1(2.0 * log_a))
    bterm = mult * (i * x).astype(jnp.float32)
    _, h = lax.associative_scan(_lin_combine, (a, bterm), axis=1)
    return h.astype(x.dtype)

def causal_pool_mixer(x, pool_w, pool_b, pool_scale):
    B, S, C = x.shape
    x32 = x.astype(jnp.float32)
    cs = jnp.pad(jnp.cumsum(x32, axis=1), ((0, 0), (1, 0), (0, 0)))
    t = jnp.arange(S)
    outs = []
    for g, w in enumerate(POOL_WINDOWS):
        lo, hi = g * POOL_GROUP_DIM, (g + 1) * POOL_GROUP_DIM
        csg = cs[..., lo:hi]
        lagged = jnp.pad(csg[:, :S + 1 - w], ((0, 0), (w - 1, 0), (0, 0)))
        count = jnp.minimum(t + 1, w).astype(jnp.float32)[None, :, None]
        outs.append((csg[:, 1:] - lagged) / count - x32[..., lo:hi])
    p = jnp.concatenate(outs, axis=-1).reshape(B, S, POOL_GROUPS, POOL_GROUP_DIM)
    y = jnp.einsum('bsgc,gcd->bsgd', p, pool_w.astype(jnp.float32)).reshape(B, S, C) + pool_b
    return (y * pool_scale).astype(x.dtype)

def clamped_swiglu(u):
    glu = jnp.minimum(u[..., ::2], SWIGLU_LIMIT)
    lin = jnp.clip(u[..., 1::2], -SWIGLU_LIMIT, SWIGLU_LIMIT)
    return glu * jax.nn.sigmoid(SWIGLU_ALPHA * glu) * (lin + 1.0)

def moe_ffn(h, router_w, router_b, w1, b1, w2, b2):
    B, S, D = h.shape
    T = B * S
    ht = h.reshape(T, D)
    logits = (ht @ router_w + router_b).astype(jnp.float32)
    top_val, top_idx = lax.top_k(logits, TOP_K)
    gates = jax.nn.softmax(top_val, axis=-1)
    flat_e = top_idx.reshape(-1).astype(jnp.int32)
    flat_tok = jnp.arange(T * TOP_K, dtype=jnp.int32) // TOP_K
    flat_w = gates.reshape(-1)
    order = jnp.argsort(flat_e)
    sorted_e = flat_e[order]
    counts = jnp.bincount(flat_e, length=N_EXPERTS).astype(jnp.int32)
    starts = jnp.cumsum(counts) - counts
    padded = (counts + EXPERT_BLOCK - 1) // EXPERT_BLOCK * EXPERT_BLOCK
    pad_ends = jnp.cumsum(padded)
    pad_starts = pad_ends - padded
    rank = jnp.arange(T * TOP_K, dtype=jnp.int32) - starts[sorted_e]
    dest = pad_starts[sorted_e] + rank
    n_blocks = -(-(T * TOP_K) // EXPERT_BLOCK) + N_EXPERTS
    cap = n_blocks * EXPERT_BLOCK
    tok_buf = jnp.full((cap,), T, dtype=jnp.int32).at[dest].set(flat_tok[order])
    w_buf = jnp.zeros((cap,), jnp.float32).at[dest].set(flat_w[order])
    block_start = jnp.arange(n_blocks, dtype=jnp.int32) * EXPERT_BLOCK
    block_e = jnp.minimum(jnp.searchsorted(pad_ends, block_start, side='right'), N_EXPERTS - 1)
    h_pad = jnp.concatenate([ht, jnp.zeros((1, D), ht.dtype)], axis=0)

    def expert_block(args):
        idx, wt, e = args
        xb = h_pad[idx]
        u = xb @ w1[e] + b1[e]
        y = clamped_swiglu(u) @ w2[e] + b2[e]
        return y.astype(jnp.float32) * wt[:, None]

    y = lax.map(expert_block, (tok_buf.reshape(n_blocks, EXPERT_BLOCK),
                               w_buf.reshape(n_blocks, EXPERT_BLOCK), block_e))
    out = jnp.zeros((T + 1, D), jnp.float32).at[tok_buf].add(y.reshape(cap, D))[:T]
    return out.reshape(B, S, D).astype(h.dtype)

def setup_inputs(seed: int = 0) -> dict:
    key = jax.random.key(seed)
    ks = jax.random.split(key, 28)
    f32 = jnp.float32
    nrm = lambda k, shape, s: jax.random.normal(k, shape, f32) * s
    gain = lambda k: 1.0 + 0.05 * jax.random.normal(k, (DEPTH, D_MODEL), f32)
    u = jax.random.uniform(ks[13], (DEPTH, LRU_WIDTH), f32, minval=0.9, maxval=0.999)
    p = u ** (1.0 / LRU_C)
    lru_lambda = jnp.log(p) - jnp.log1p(-p)
    return {
        "x": nrm(ks[0], (BATCH, SEQ, D_MODEL), 1.0),
        "c": nrm(ks[1], (BATCH, D_MODEL), 1.0),
        "w_ada": nrm(ks[2], (DEPTH, D_MODEL, 6 * D_MODEL), D_MODEL ** -0.5),
        "b_ada": nrm(ks[3], (DEPTH, 6 * D_MODEL), 0.02),
        "norm_mix_pre": gain(ks[4]),
        "norm_mix_post": gain(ks[5]),
        "w_in": nrm(ks[6], (DEPTH, D_MODEL, IN_WIDTH), D_MODEL ** -0.5),
        "conv_w": nrm(ks[7], (DEPTH, CONV_WIDTH, LRU_WIDTH), CONV_WIDTH ** -0.5),
        "conv_b": nrm(ks[8], (DEPTH, LRU_WIDTH), 0.02),
        "gate_a_w": nrm(ks[9], (DEPTH, LRU_HEADS, LRU_HEAD_DIM, LRU_HEAD_DIM), LRU_HEAD_DIM ** -0.5),
        "gate_a_b": nrm(ks[10], (DEPTH, LRU_WIDTH), 0.02),
        "gate_x_w": nrm(ks[11], (DEPTH, LRU_HEADS, LRU_HEAD_DIM, LRU_HEAD_DIM), LRU_HEAD_DIM ** -0.5),
        "gate_x_b": nrm(ks[12], (DEPTH, LRU_WIDTH), 0.02),
        "lru_lambda": lru_lambda,
        "pool_w": nrm(ks[14], (DEPTH, POOL_GROUPS, POOL_GROUP_DIM, POOL_GROUP_DIM), POOL_GROUP_DIM ** -0.5),
        "pool_b": nrm(ks[15], (DEPTH, POOL_WIDTH), 0.02),
        "pool_scale": 1.0 + 0.05 * jax.random.normal(ks[16], (DEPTH, POOL_WIDTH), f32),
        "w_out": nrm(ks[17], (DEPTH, MIX_WIDTH, D_MODEL), MIX_WIDTH ** -0.5),
        "norm_ffn_pre": gain(ks[18]),
        "norm_ffn_post": gain(ks[19]),
        "router_w": nrm(ks[20], (DEPTH, D_MODEL, N_EXPERTS), D_MODEL ** -0.5),
        "router_b": nrm(ks[21], (DEPTH, N_EXPERTS), 0.01),
        "expert_w1": nrm(ks[22], (DEPTH, N_EXPERTS, D_MODEL, 2 * D_EXPERT), D_MODEL ** -0.5),
        "expert_b1": nrm(ks[23], (DEPTH, N_EXPERTS, 2 * D_EXPERT), 0.02),
        "expert_w2": nrm(ks[24], (DEPTH, N_EXPERTS, D_EXPERT, D_MODEL), D_EXPERT ** -0.5),
        "expert_b2": nrm(ks[25], (DEPTH, N_EXPERTS, D_MODEL), 0.02),
    }

def reference(x, c, w_ada, b_ada, norm_mix_pre, norm_mix_post, w_in, conv_w, conv_b,
              gate_a_w, gate_a_b, gate_x_w, gate_x_b, lru_lambda, pool_w, pool_b, pool_scale,
              w_out, norm_ffn_pre, norm_ffn_post, router_w, router_b,
              expert_w1, expert_b1, expert_w2, expert_b2):
    c_act = jax.nn.silu(c)
    for l in range(DEPTH):
        mod = c_act @ w_ada[l] + b_ada[l]
        shift_m, scale_m, gate_m, shift_f, scale_f, gate_f = jnp.split(mod, 6, axis=-1)

        h = modulate(rms_norm(x, norm_mix_pre[l]), shift_m, scale_m)
        u = h @ w_in[l]
        xa = u[..., :LRU_WIDTH]
        ga = u[..., LRU_WIDTH:2 * LRU_WIDTH]
        xb = u[..., 2 * LRU_WIDTH:]
        xa = causal_depthwise_conv(xa, conv_w[l], conv_b[l])
        ya = rg_lru(xa, gate_a_w[l], gate_a_b[l], gate_x_w[l], gate_x_b[l], lru_lambda[l]) * jax.nn.gelu(ga)
        yb = causal_pool_mixer(xb, pool_w[l], pool_b[l], pool_scale[l])
        mix = jnp.concatenate([ya, yb], axis=-1) @ w_out[l]
        x = x + gate_m[:, None, :] * rms_norm(mix, norm_mix_post[l])

        h = modulate(rms_norm(x, norm_ffn_pre[l]), shift_f, scale_f)
        f = moe_ffn(h, router_w[l], router_b[l], expert_w1[l], expert_b1[l], expert_w2[l], expert_b2[l])
        x = x + gate_f[:, None, :] * rms_norm(f, norm_ffn_post[l])
    return x


_drawn_inputs = setup_inputs


def setup_inputs(seed=0):
    import zlib

    import numpy as np

    out = dict(_drawn_inputs(seed))
    spreads = {}
    factors = {'gate_a_b': 5.559,
     'gate_x_b': 4.89,
     'pool_b': 3.29,
     'router_b': 3.249,
     'expert_b1': 5.988,
     'expert_b2': 8.0}
    for name, (base, spread) in spreads.items():
        noise = np.random.default_rng([zlib.crc32(name.encode()), seed]).standard_normal(out[name].shape)
        drawn = base * np.exp(spread * noise) if base else spread * noise
        out[name] = __import__('jax').numpy.asarray(drawn.astype(out[name].dtype))
    for name, factor in factors.items():
        out[name] = (out[name] * factor).astype(out[name].dtype)
    return out
```

```python
import concourse.bass as bass
from concourse import mybir
from contextlib import ExitStack


def hybrid_layer(nc, x, c, w_ada, b_ada, norm_mix_pre, norm_mix_post, w_in, conv_w, conv_b, gate_a_w, gate_a_b,
                 gate_x_w, gate_x_b, lru_lambda, pool_w, pool_b, pool_scale, w_out, norm_ffn_pre, norm_ffn_post,
                 router_w, router_b, expert_w1, expert_b1, expert_w2, expert_b2, out):
    fp32, i32, u32 = mybir.dt.float32, mybir.dt.int32, mybir.dt.uint32
    ALU, ACT, AX = mybir.AluOpType, mybir.ActivationFunctionType, mybir.AxisListType

    P = 128
    T, D = x.shape[1], x.shape[2]
    TT = T // P
    KT = D // P
    E, F2 = expert_w1.shape[1], expert_w1.shape[3]
    F = F2 // 2
    TOPK = 4
    FT = w_in.shape[2] // P // 3
    CONV = conv_w.shape[1]
    LRU_C, EPS, LIMIT, ALPHA = 8.0, 1e-6, 7.0, 1.702
    J = 4
    H = 32
    QW = D // J
    QM = QW // P
    UW = F2 // J
    STEPS_MAX = T * TOPK // (2 * H) + E
    NQ = 2 * STEPS_MAX + 4
    EMPTY = 1 << 20
    PADC, PADP = CONV - 1, 15

    h_rows = nc.dram_tensor("h_rows", (T * J, QW), fp32).ap()
    y_rows = nc.dram_tensor("y_rows", (T * TOPK * J, QW), fp32).ap()
    h_store = h_rows.rearrange("(t j) c -> t (j c)", j=J)
    y_load = y_rows.rearrange("(t r) c -> t (r c)", r=TOPK * J)

    w_ada_v = w_ada[0].rearrange("(k p) n -> p k n", p=P)
    w_in_v = w_in[0].rearrange("(k p) n -> p k n", p=P)
    w_out_v = w_out[0].rearrange("(k p) n -> p k n", p=P)
    w1_v = expert_w1[0].rearrange("e (k p) n -> e p k n", p=P)
    w2_v = expert_w2[0].rearrange("e (k p) n -> e p k n", p=P)

    ctx = ExitStack()
    with ctx:
        def sb(name, shape, dt=fp32):
            return ctx.enter_context(nc.sbuf_tensor(name, shape, dt))

        def sem(name):
            return ctx.enter_context(nc.semaphore(name))

        def sems(name, n):
            return [sem(f"{name}{i}") for i in range(n)]

        W1 = sb("W1", [P, 2, KT, F2])
        W2 = sb("W2", [P, KT, D])
        OV = sb("OV", [P, 6656])
        x1 = sb("x1", [P, TT, D])
        gate_f_bc = sb("gate_f_bc", [P, D])
        ident = sb("ident", [P, P])
        ones = sb("ones", [P, P])
        gates = sb("gates", [P, TT, TOPK])
        counts = sb("counts", [1, 2, E], i32)
        src_cur = sb("src_cur", [P, 2], i32)
        dst_cur = [sb("dst_cur_a", [P, 1], i32), sb("dst_cur_b", [P, 1], i32)]
        stat = sb("stat", [P, 8, TT])
        router_bias = sb("router_bias", [P, E])

        def carver(area):
            at = [0]

            def take(*shape):
                n = 1
                for size in shape:
                    n *= size
                v = area[:, at[0]:at[0] + n]
                at[0] += n
                assert at[0] <= area.shape[1], (at[0], area.shape)
                if len(shape) > 1:
                    names = "abcd"[:len(shape)]
                    v = v.rearrange(f"p ({' '.join(names)}) -> p {' '.join(names)}", **dict(zip(names, shape)))
                return v
            return take

        def flat(v):
            return v.rearrange("p a b -> p (a b)")

        HALF = KT // 2
        A_lo, A_hi = flat(W1[:, 0, 0:HALF, :]), flat(W1[:, 0, HALF:KT, :])
        B_lo, B_hi = flat(W1[:, 1, 0:HALF, :]), flat(W1[:, 1, HALF:KT, :])

        ADA_RING, AK = 3, 2
        take = carver(A_lo)
        ada_ring = take(ADA_RING, AK, D)
        gate_bd = take(2, FT, P)
        pool_sb = take(FT, P)
        inv_count = take(PADP + 1)
        mod_col = take(2, J, QM)
        lru_c = take(8, FT)
        pool_pb = take(FT)
        c_sig = take(KT)
        take = carver(A_hi)
        conv_x = take(FT, T)
        rgate = take(T)
        igate = take(2, T)
        decay = take(2, T)
        decay2 = take(2, T)
        tanh_m = take(2, T)
        xa_pad = take(2, T + PADC)
        c_rep = take(KT, H)
        cols = take(48)
        win_ring = carver(B_lo)(2, KT, FT * P)
        take = carver(B_lo)
        mixb = take(2, D)
        junk = take(D)
        hn = take(2, D)
        h2T = take(2, KT, P)
        take = carver(B_hi)
        hT = take(KT, T)
        xb_pad = take(2, T + PADP)
        sums = take(2, T + PADP)
        ga = take(2, T)
        gel = take(T)
        B_HI = B_hi.shape[1]
        router_sb = carver(B_hi[:, B_HI - KT * E:])(KT, E)
        vec_rows = carver(B_hi[:, B_HI - KT * E - P:])(P)
        bc = carver(B_hi[:, KT * T:])(3, D)
        TK = TT * TOPK
        take = carver(B_hi)
        slot_val = take(TK, 2, NQ)
        hot_t = take(TK, P)
        hot_e = take(TT, TOPK, E)
        route_tmp = take(TK, E)
        catT = carver(OV)(KT, T)
        xn = carver(OV)(TT, D)
        take = carver(OV[:, KT * T:])
        ada_rows = take(6, QW)
        gain_rows = take(4, QW)
        take = carver(OV[:, KT * T:])
        iota_q = take(NQ)
        iota_t = take(P)
        iota_e = take(E)
        upper = take(P)
        tok_no = take(2, TK)
        j_off = take(1)
        logits = take(TT, E)
        top = take(TT, 8)
        top_i = take(TT, 8).bitcast(u32)
        sel = take(TT, E)
        slot_e = take(TT, E)
        exp_f = take(4, E)
        exp_i = take(3, E).bitcast(i32)
        tk_f = take(4, TK)
        tk_i = take(3, TK).bitcast(i32)
        top_d = take(TT, TOPK)
        top_e = take(TT, TOPK)
        idx_f = take(2 * NQ)
        idx_e = take(2 * NQ)
        take = carver(OV)
        xg = [take(QW), take(QW)]
        xT = take(2, QM, P)
        b1_bc = take(2, UW)
        b2_bc = take(2, QW)
        u_sb = take(2, UW)
        glu = take(2, QW)
        lin = take(2, QW)
        sig = take(2, QW)
        gT = take(2, QM, P)
        y_sb = [take(QW), take(QW)]
        idx = take(2, NQ // 2, 2).bitcast(i32)
        y_all = carver(flat(W1[:, 0, :, :]))(TT, TOPK, D)
        fin = carver(B_lo)(TT, D)
        fin_junk = carver(B_hi)(D)

        bank = [ctx.enter_context(nc.psum_tensor(f"bank{i}", [P, 512], fp32)) for i in range(8)]
        R = 4

        order = [("xT", k) for k in range(KT)] + [("xa", f) for f in range(FT)] + [("xb", f) for f in range(FT)]
        for f in range(FT):
            order += [("r", f), ("i", f), ("ga", f)]
        order += [("pool", f) for f in range(FT)]
        for i in range(TT):
            order += [("mix", i, 0), ("mix", i, 1)]
            if i >= 1:
                order += [("hT", i - 1, 0), ("hT", i - 1, 1), ("logits", i - 1)]
        order += [("hT", TT - 1, 0), ("hT", TT - 1, 1), ("logits", TT - 1)]
        number = {what: n for n, what in enumerate(order)}

        x_in = sems("x_in", TT)
        vec_in = sem("vec_in")
        ada_in = sems("ada_in", ADA_RING)
        win_in = sems("win_in", 2)
        wout_in = sem("wout_in")
        rows_in = sem("rows_in")
        bd_in = sem("bd_in")
        pool_in = sem("pool_in")
        router_in = sem("router_in")
        window_ok = sem("window_ok")
        pool_const = sem("pool_const")
        ident_ok = sem("ident_ok")
        pads_ok = sem("pads_ok")
        x_sq = sem("x_sq")
        xn_ok = sem("xn_ok")
        vecT_ok = sem("vecT_ok")
        cols_ok = sem("cols_ok")
        c_sig_ok = sem("c_sig_ok")
        c_ok = sem("c_ok")
        lam_abs_ok = sem("lam_abs_ok")
        lam_exp_ok = sem("lam_exp_ok")
        lru_c_ok = sem("lru_c_ok")
        ada_used = sem("ada_used")
        mod_row = sem("mod_row")
        mod_colT = sem("mod_colT")
        mod_col_ok = sem("mod_col_ok")
        prod = sem("prod")
        evac = sem("evac")
        conv_ok = sem("conv_ok")
        pool_ok = sem("pool_ok")
        lru_in = sem("lru_in")
        lru_ok = sem("lru_ok")
        gel_in = sem("gel_in")
        gel_sig = sem("gel_sig")
        gel_ok = sem("gel_ok")
        bc_ps = sem("bc_ps")
        bc_ok = sem("bc_ok")
        x1_ok = sem("x1_ok")
        x1_sq = sem("x1_sq")
        hn_ok = sem("hn_ok")
        h_stored = sems("h_stored", 2)
        route_const = sem("route_const")
        sel_ok = sem("sel_ok")
        rank_ok = sem("rank_ok")
        top_ok = sem("top_ok")
        top_exp = sem("top_exp")
        counts_ok = sem("counts_ok")
        slots_ok = sem("slots_ok")
        table_ok = sem("table_ok")
        idx_ok = sem("idx_ok")
        ms_ok = sem("ms_ok")
        rms_ok = sem("rms_ok")
        m2_ok = sem("m2_ok")
        root_ok = sem("root_ok")
        apart_n = sem("apart_n")
        dve_chain = sem("dve_chain")
        act_chain = sem("act_chain")
        pool_chain = sem("pool_chain")
        w1_in = [sems(f"w1_in{s}_", 4) for s in range(2)]
        w2_in = sems("w2_in", 2)
        bias_in = sems("bias_in", 2)
        expert_done = sem("expert_done")
        bias_done = sem("bias_done")
        xg_in = sem("xg_in")
        xT_ps = sem("xT_ps")
        xT_ok = sem("xT_ok")
        u_ps = sems("u_ps", 2)
        u_ok = sems("u_ok", 2)
        lin_ok = sems("lin_ok", 2)
        glu_ok = sems("glu_ok", 2)
        sig_ok = sems("sig_ok", 2)
        mul_ok = sems("mul_ok", 2)
        act_ok = sems("act_ok", 2)
        gT_ps = sems("gT_ps", 2)
        gT_ok = sems("gT_ok", 2)
        y_ps = sems("y_ps", 2)
        y_ok = sems("y_ok", 2)
        y_stored = sems("y_stored", 2)
        src_ok = sem("src_ok")
        dst_ok = sems("dst_ok", 2)
        moe_done = sem("moe_done")
        y_in = sems("y_in", TT)
        y_first = sem("y_first")
        f_sum = sem("f_sum")
        f_sq = sem("f_sq")
        out_ok = sem("out_ok")
        out_stored = sem("out_stored")

        f_chain = sem("f_chain")
        COL = {name: CONV * FT + n * FT for n, name in enumerate(
            ("conv_b", "gate_a_b", "gate_x_b", "lru_lambda", "pool_b", "pool_scale", "c"))}
        c_col = cols[:, COL["c"]:COL["c"] + KT]
        gT_bank = [bank[3], bank[6]]
        GELU = 2.0 * (2.0 / 3.141592653589793) ** 0.5

        def col(name, f):
            return cols[:, COL[name] + f:COL[name] + f + 1]

        def flat3(v):
            return v.rearrange("p a b c -> p (a b c)")

        block = ctx.enter_context(nc.Block())

        def apart(engine):
            engine.sem_inc(apart_n, 1)

        def linker(engine, chain):
            n = [0]

            def link(instruction):
                n[0] += 1
                instruction.then_inc(chain, 1)
                engine.wait_ge(chain, n[0])
            return link

        CHUNK = KT // 4

        def w1_part(e, ch):
            return w1_v[bass.ds(e, 1), :, ch * CHUNK:(ch + 1) * CHUNK, :].rearrange("e p k n -> p (e k) n")

        def load_w1(sp, e, slot, ch):
            sp.dma_start(W1[:, slot, ch * CHUNK:(ch + 1) * CHUNK, :], w1_part(e, ch)).then_inc(w1_in[slot][ch], 16)

        def load_w2(sp, e):
            for hf in range(2):
                src = w2_v[bass.ds(e, 1), :, hf * HALF:(hf + 1) * HALF, :].rearrange("e p k n -> p (e k) n")
                sp.dma_start(W2[:, hf * HALF:(hf + 1) * HALF, :], src).then_inc(w2_in[hf], 16)

        def load_bias(sp, e, slot):
            for j in range(J):
                part = slice(H * j, H * j + H)
                sp.dma_start(b1_bc[part, slot, :], expert_b1[0, bass.ds(e, 1), UW * j:UW * j + UW]
                             .to_broadcast([H, UW])).then_inc(bias_in[slot], 16)
                sp.dma_start(b2_bc[part, slot, :], expert_b2[0, bass.ds(e, 1), QW * j:QW * j + QW]
                             .to_broadcast([H, QW])).then_inc(bias_in[slot], 16)
        BIAS_INC = 2 * J * 16

        @block.sync
        def _(sp):
            for i in range(TT):
                sp.dma_start(x1[:, i, :], x[0, i * P:(i + 1) * P, :]).then_inc(x_in[i], 16)

            def load_ada(n):
                v, kk = n // (KT // AK), n % (KT // AK)
                if n >= ADA_RING:
                    sp.wait_ge(ada_used, n - ADA_RING + 1)
                sp.dma_start(ada_ring[:, n % ADA_RING, :, :],
                             w_ada_v[:, kk * AK:(kk + 1) * AK, v * D:(v + 1) * D]).then_inc(ada_in[n % ADA_RING], 16)

            def load_win(part, slot):
                sp.dma_start(win_ring[:, slot, :, :], w_in_v[:, :, part * FT * P:(part + 1) * FT * P])\
                    .then_inc(win_in[slot], 16)

            PIECES = KT // AK
            for n in range(2 * PIECES):
                load_ada(n)
            load_win(0, 0)
            load_win(2, 1)
            for n in range(2 * PIECES, 3 * PIECES):
                load_ada(n)
            sp.wait_ge(prod, number["xa", FT - 1] + 1)
            load_win(1, 0)
            sp.dma_start(W2[:, :, :], w_out_v).then_inc(wout_in, 16)
            for n in range(3 * PIECES, 6 * PIECES):
                load_ada(n)
            sp.wait_ge(evac, number["pool", FT - 1] + 1)
            sp.wait_ge(ada_used, 6 * PIECES)
            sp.wait_ge(lru_ok, FT)
            for ch in range(4):
                load_w1(sp, 0, 0, ch)
            sp.wait_ge(prod, number["mix", TT - 1, 1] + 1)
            load_w2(sp, 0)
            sp.wait_ge(idx_ok, 1)
            load_bias(sp, 0, 0)
            load_bias(sp, 1, 1)
            for s in range(2):
                sp.wait_ge(h_stored[s], 16 * TT // 2)
            for ch in range(4):
                load_w1(sp, 1, 1, ch)
            sp.wait_ge(expert_done, 1)
            load_w2(sp, 1)
            with sp.Fori(1, E // 2) as pair:
                for slot in range(2):
                    e = 2 * pair + slot
                    sp.wait_ge(expert_done, e - 1)
                    for ch in range(4):
                        load_w1(sp, e, slot, ch)
                    sp.wait_ge(bias_done, e - 1)
                    load_bias(sp, e, slot)
                    sp.wait_ge(expert_done, e)
                    load_w2(sp, e)
            sp.wait_ge(moe_done, 1)
            for i in range(TT):
                sp.dma_start(y_all[:, i, :, :].rearrange("p k d -> p (k d)"), y_load[i * P:(i + 1) * P, :])\
                    .then_inc(y_in[i], 16)
            for i in range(TT):
                sp.wait_ge(out_ok, i + 1)
                sp.dma_start(out[0, i * P:(i + 1) * P, :], fin[:, i, :]).then_inc(out_stored, 16)
            sp.wait_ge(out_stored, 16 * TT)

        @block.gpsimd
        def _(pool):
            link = linker(pool, pool_chain)
            link(nc.gpsimd.memset(ident[:, :], 0.0))
            nc.gpsimd.affine_select(out=ident[:, :], in_=ident[:, :], compare_op=ALU.not_equal, fill=1.0, base=0,
                                    pattern=[[-1, P]], channel_multiplier=1).then_inc(ident_ok, 1)
            nc.gpsimd.memset(ones[:, :], 1.0).then_inc(ident_ok, 1)
            for j in range(J):
                part = slice(H * j, H * j + H)
                src = b_ada[0:1, :].rearrange("a (v q c) -> a q v c", v=6, q=J)[:, j, :, :]
                pool.dma_start(ada_rows[part, :, :], src.to_broadcast([H, 6, QW])).then_inc(rows_in, 16)
                for g, gain in enumerate((norm_mix_pre, norm_mix_post, norm_ffn_pre, norm_ffn_post)):
                    pool.dma_start(gain_rows[part, g, :], gain[0:1, QW * j:QW * j + QW].to_broadcast([H, QW]))\
                        .then_inc(rows_in, 16)
            link(nc.gpsimd.memset(gate_bd[:, :, :, :], 0.0))
            for n, w in enumerate((gate_a_w, gate_x_w)):
                for par in range(2):
                    lo = par * (P // 2)
                    pool.dma_start(gate_bd[lo:lo + P // 2, n, :, lo:lo + P // 2],
                                   w[0].rearrange("(f r) i o -> r i f o", r=2)[par]).then_inc(bd_in, 16)
            pool.dma_start(pool_sb, pool_w[0].rearrange("g c d -> c g d")).then_inc(pool_in, 16)
            pool.dma_start(router_sb, router_w[0].rearrange("(k p) e -> p k e", p=P)).then_inc(router_in, 16)
            pool.dma_start(router_bias[:, :], router_b[0:1, :].to_broadcast([P, E])).then_inc(router_in, 16)
            nc.gpsimd.memset(xb_pad[:, :, 0:PADP], 0.0).then_inc(pads_ok, 1)
            nc.gpsimd.iota(inv_count, [[1, PADP + 1]], base=1, channel_multiplier=0,
                           allow_small_or_imprecise_dtypes=True).then_inc(window_ok, 1)
            pool.wait_ge(pool_const, 1)
            L = T + PADP
            for g in range(FT):
                w = 2 ** (g + 1)
                pool.wait_ge(evac, number["xb", g] + 1)
                cur = xb_pad[:, g % 2, :]
                for level in range(g + 1):
                    s, lo = 2 ** level, 2 ** (level + 1) - 1
                    nxt = sums[:, level % 2, :]
                    link(nc.gpsimd.tensor_tensor(nxt[:, lo:L], cur[:, lo:L], cur[:, lo - s:L - s], ALU.add))
                    cur = nxt
                p_out, xb = catT[:, FT + g, :], xb_pad[:, g % 2, PADP:L]
                link(nc.gpsimd.tensor_scalar(p_out, cur[:, PADP:L], 1.0 / w, None, ALU.mult))
                link(nc.gpsimd.tensor_tensor(p_out[:, 0:w - 1], cur[:, PADP:PADP + w - 1], inv_count[:, 0:w - 1], ALU.mult))
                nc.gpsimd.tensor_tensor(p_out, p_out, xb, ALU.subtract).then_inc(pool_ok, 1)
                pool.wait_ge(pool_ok, g + 1)
            pool.wait_ge(bc_ps, 4)
            IMP = dict(allow_small_or_imprecise_dtypes=True)
            nc.gpsimd.iota(iota_q, [[1, NQ]], base=0, channel_multiplier=0, **IMP).then_inc(route_const, 1)
            nc.gpsimd.iota(iota_t, [[0, J], [1, H]], base=0, channel_multiplier=0, **IMP).then_inc(route_const, 1)
            nc.gpsimd.iota(iota_e, [[1, E]], base=0, channel_multiplier=0, **IMP).then_inc(route_const, 1)
            nc.gpsimd.iota(tok_no[:, 0, :], [[P, TT], [0, TOPK]], base=1, channel_multiplier=1, **IMP)\
                .then_inc(route_const, 1)
            nc.gpsimd.iota(tok_no[:, 1, :], [[P * TOPK, TT], [1, TOPK]], base=1, channel_multiplier=TOPK, **IMP)\
                .then_inc(route_const, 1)
            link(nc.gpsimd.memset(upper, 1.0))
            nc.gpsimd.affine_select(out=upper, in_=upper, compare_op=ALU.is_gt, fill=0.0, base=0,
                                    pattern=[[1, P]], channel_multiplier=-1).then_inc(route_const, 1)
            for i in range(TT):
                pool.wait_ge(hn_ok, i + 1)
                pool.dma_start(h_store[i * P:(i + 1) * P, :], hn[:, i % 2, :]).then_inc(h_stored[i % 2], 16)
            for s in range(2):
                pool.wait_ge(h_stored[s], 16 * TT // 2)
            pool.wait_ge(idx_ok, 1)
            link(nc.gpsimd.memset(xg[0], 0.0))
            link(nc.gpsimd.memset(xg[1], 0.0))

            def gather(step):
                nc.gpsimd.tensor_copy(src_cur[:, :].rearrange("p (a b) -> p a b", a=1), idx[:, 0, bass.ds(step, 1), :])\
                    .then_inc(src_ok, 1)
                pool.wait_ge(src_ok, step + 1)
                apart(pool)
                for hf in range(2):
                    pool.indirect_dma_start(xg[hf], None, h_rows, bass.IndirectOffsetOnAxis(ap=src_cur[:, hf:hf + 1], axis=0),
                                            bounds_check=T * J - 1, oob_is_err=False).then_inc(xg_in, 16)

            def scatter(hf, n, step):
                pool.wait_ge(y_ok[hf], n + 1)
                nc.gpsimd.tensor_copy(dst_cur[hf][:, :].rearrange("p (a b) -> p a b", a=1),
                                      idx[:, 1, bass.ds(step, 1), hf:hf + 1]).then_inc(dst_ok[hf], 1)
                pool.wait_ge(dst_ok[hf], n + 1)
                apart(pool)
                pool.indirect_dma_start(y_rows, bass.IndirectOffsetOnAxis(ap=dst_cur[hf][:, 0:1], axis=0), y_sb[hf], None,
                                        bounds_check=T * TOPK * J - 1, oob_is_err=False).then_inc(y_stored[hf], 16)

            for hf in range(2):
                nc.gpsimd.memset(y_sb[hf], 0.0).then_inc(y_ok[hf], 1)
                scatter(hf, 0, NQ // 2 - 1)
            gather(0)
            step, full = pool.alloc_register("pool_step"), pool.alloc_register("pool_full")
            pool.reg_mov(step, 0)
            pool.reg_mov(full, 0)
            with pool.Fori(0, E) as e:
                n_steps = pool.value_load(counts[0:1, 0, bass.ds(e, 1)], min_val=0, max_val=T // (2 * H))
                n_halves = pool.value_load(counts[0:1, 1, bass.ds(e, 1)], min_val=0, max_val=T // H)
                with pool.If(n_steps > 0):
                    with pool.Fori(0, n_steps) as k:
                        s = pool.snap(step, min_val=0, max_val=STEPS_MAX)
                        pool.wait_ge(xT_ps, s + 1)
                        apart(pool)
                        gather(s + 1)
                        scatter(0, s + 1, s)
                        with pool.If(2 * k + 1 < n_halves):
                            n = pool.snap(full, min_val=0, max_val=STEPS_MAX)
                            scatter(1, n + 1, s)
                            pool.reg_add(full, full, 1)
                        pool.reg_add(step, step, 1)
                pool.nop()
            s = pool.snap(step, min_val=0, max_val=STEPS_MAX)
            n = pool.snap(full, min_val=0, max_val=STEPS_MAX)
            pool.wait_ge(y_stored[0], 16 * s + 16)
            pool.wait_ge(y_stored[1], 16 * n + 16)
            apart(pool)
            pool.drain().then_inc(moe_done, 1)

        @block.scalar
        def _(act):
            link = linker(act, act_chain)
            vecs = [(0, conv_w[0].rearrange("k (f p) -> (k f) p", p=P))]
            at = CONV * FT
            for v in (conv_b, gate_a_b, gate_x_b, lru_lambda, pool_b, pool_scale):
                vecs.append((at, v[0].rearrange("(f p) -> f p", p=P)))
                at += FT
            vecs.append((at, c[0].rearrange("(k p) -> k p", p=P)))
            for at, v in vecs:
                act.dma_start(vec_rows[at:at + v.shape[0], :], v).then_inc(vec_in, 16)
            act.wait_ge(cols_ok, 1)
            nc.scalar.activation(c_sig, c_col, ACT.Sigmoid).then_inc(c_sig_ok, 1)
            act.wait_ge(lam_abs_ok, 1)
            nc.scalar.activation(lru_c[:, 1, :], lru_c[:, 0, :], ACT.Exp, scale=-1.0).then_inc(lam_exp_ok, 1)
            for i in range(TT):
                act.wait_ge(x_in[i], 16)
                nc.scalar.activation(hT[:, 2 * i:2 * i + 2, :].rearrange("p a b -> p (a b)"), x1[:, i, :], ACT.Square,
                                     accum_out=stat[:, 0, i:i + 1]).then_inc(x_sq, 1)
            roots = [0]

            def root(v):
                roots[0] += 1
                act.wait_ge(ms_ok, roots[0])
                nc.scalar.activation(v, v, ACT.Sqrt).then_inc(rms_ok, 1)

            for i in range(TT):
                root(stat[:, 1, i:i + 1])

            def take_out(what):
                n = number[what]
                act.wait_ge(prod, n + 1)
                return bank[n % R]

            act.wait_ge(mod_col_ok, 1)
            act.wait_ge(x_sq, TT)
            for k in range(KT):
                ps = take_out(("xT", k))
                nc.scalar.activation(hT[:, k, :], ps[:, :], ACT.Identity, bias=mod_col[:, 0, k // QM, k % QM:k % QM + 1],
                                     scale=mod_col[:, 1, k // QM, k % QM:k % QM + 1]).then_inc(evac, 1)
            for f in range(FT):
                ps = take_out(("xa", f))
                if f >= 2:
                    act.wait_ge(conv_ok, f - 1)
                nc.scalar.activation(xa_pad[:, f % 2, PADC:], ps[:, :], ACT.Copy).then_inc(evac, 1)
            act.wait_ge(pads_ok, 1)
            for f in range(FT):
                ps = take_out(("xb", f))
                if f >= 2:
                    act.wait_ge(pool_ok, f - 1)
                nc.scalar.activation(xb_pad[:, f % 2, PADP:], ps[:, :], ACT.Copy).then_inc(evac, 1)
            act.wait_ge(lru_c_ok, 1)
            for f in range(FT):
                ps = take_out(("r", f))
                if f:
                    act.wait_ge(lru_in, 3 * f)
                nc.scalar.activation(rgate, ps[:, :], ACT.Sigmoid, bias=col("gate_a_b", f)).then_inc(evac, 1)
                ps = take_out(("i", f))
                if f >= 2:
                    act.wait_ge(lru_ok, f - 1)
                nc.scalar.activation(igate[:, f % 2, :], ps[:, :], ACT.Sigmoid, bias=col("gate_x_b", f)).then_inc(evac, 1)
                act.wait_ge(evac, number["i", f] + 1)
                nc.scalar.activation(decay[:, f % 2, :], rgate, ACT.Exp, scale=lru_c[:, 5, f:f + 1]).then_inc(lru_in, 1)
                nc.scalar.activation(decay2[:, f % 2, :], rgate, ACT.Exp, scale=lru_c[:, 6, f:f + 1]).then_inc(lru_in, 1)
                nc.scalar.activation(tanh_m[:, f % 2, :], rgate, ACT.Tanh, scale=lru_c[:, 7, f:f + 1]).then_inc(lru_in, 1)
                act.wait_ge(m2_ok, f + 1)
                nc.scalar.activation(tanh_m[:, f % 2, :], tanh_m[:, f % 2, :], ACT.Sqrt).then_inc(root_ok, 1)
                ps = take_out(("ga", f))
                if f >= 2:
                    act.wait_ge(gel_ok, f - 1)
                nc.scalar.activation(ga[:, f % 2, :], ps[:, :], ACT.Copy).then_inc(evac, 1)
                if f >= 1:
                    act.wait_ge(gel_in, f)
                    nc.scalar.activation(gel, gel, ACT.Sigmoid, scale=GELU).then_inc(gel_sig, 1)
            act.wait_ge(gel_in, FT)
            nc.scalar.activation(gel, gel, ACT.Sigmoid, scale=GELU).then_inc(gel_sig, 1)
            for f in range(FT):
                ps = take_out(("pool", f))
                nc.scalar.activation(catT[:, FT + f, :], ps[:, :], ACT.Identity, bias=pool_pb[:, f:f + 1],
                                     scale=col("pool_scale", f)).then_inc(evac, 1)

            bc_to = [bc[:, 0, :], bc[:, 1, :], bc[:, 2, :], gate_f_bc[:, :]]
            mixes = 0
            for what in order[number["mix", 0, 0]:]:
                ps = take_out(what)
                i = what[1]
                if what[0] == "mix":
                    n = what[2]
                    if i >= 2:
                        act.wait_ge(x1_ok, i - 1)
                    link(nc.scalar.activation(junk[:, 0:512], ps[:, :], ACT.Square, accum_out=stat[:, 2 + n, i:i + 1]))
                    nc.scalar.activation(mixb[:, i % 2, n * 512:(n + 1) * 512], ps[:, :], ACT.Copy).then_inc(evac, 1)
                    if n == 1:
                        if i == 0:
                            for v in range(4):
                                act.wait_ge(bc_ps, v + 1)
                                nc.scalar.activation(bc_to[v][:, 0:512], bank[4][:, :], ACT.Copy).then_inc(bc_ok, 1)
                                nc.scalar.activation(bc_to[v][:, 512:D], bank[5][:, :], ACT.Copy).then_inc(bc_ok, 1)
                        root(stat[:, 4, i:i + 1])
                        act.wait_ge(x1_ok, i + 1)
                        nc.scalar.activation(junk, x1[:, i, :], ACT.Square, accum_out=stat[:, 5, i:i + 1])\
                            .then_inc(x1_sq, 1)
                        act.wait_ge(x1_sq, i + 1)
                        root(stat[:, 6, i:i + 1])
                elif what[0] == "hT":
                    n = what[2]
                    nc.scalar.activation(h2T[:, i % 2, n * HALF:(n + 1) * HALF, :].rearrange("p a b -> p (a b)"), ps[:, :],
                                         ACT.Copy).then_inc(evac, 1)
                else:
                    nc.scalar.activation(logits[:, i, :], ps[:, 0:E], ACT.Copy).then_inc(evac, 1)
            act.wait_ge(top_ok, 1)
            nc.scalar.activation(top_e, top_d, ACT.Exp).then_inc(top_exp, 1)

            act.preload_act_table(ACT.Sigmoid)

            def take_xT(s):
                act.wait_ge(xT_ps, s + 1)
                nc.scalar.activation(flat3(xT), bank[2][:, :], ACT.Copy).then_inc(xT_ok, 1)

            def sigmoid(hf, n):
                act.wait_ge(glu_ok[hf], n + 1)
                nc.scalar.activation(sig[:, hf, :], glu[:, hf, :], ACT.Sigmoid, scale=ALPHA).then_inc(sig_ok[hf], 1)

            def take_gT(hf, n):
                act.wait_ge(gT_ps[hf], n + 1)
                nc.scalar.activation(flat(gT[:, hf, :, :]), gT_bank[hf][:, 0:QW], ACT.Copy).then_inc(gT_ok[hf], 1)

            take_xT(0)
            act.wait_ge(counts_ok, 2)
            step, full = act.alloc_register("act_step"), act.alloc_register("act_full")
            act.reg_mov(step, 0)
            act.reg_mov(full, 0)
            with act.Fori(0, E) as e:
                n_steps = act.value_load(counts[0:1, 0, bass.ds(e, 1)], min_val=0, max_val=T // (2 * H))
                n_halves = act.value_load(counts[0:1, 1, bass.ds(e, 1)], min_val=0, max_val=T // H)
                with act.If(n_steps > 0):
                    with act.Fori(0, n_steps) as k:
                        s = act.snap(step, min_val=0, max_val=STEPS_MAX)
                        n = act.snap(full, min_val=0, max_val=STEPS_MAX)
                        sigmoid(0, s)
                        with act.If(2 * k + 1 < n_halves):
                            sigmoid(1, n)
                        take_xT(s + 1)
                        take_gT(0, s)
                        with act.If(2 * k + 1 < n_halves):
                            take_gT(1, n)
                            act.reg_add(full, full, 1)
                        act.reg_add(step, step, 1)
                act.nop()

            for i in range(TT):
                act.wait_ge(y_in[i], 16)
                nc.scalar.activation(fin[:, i, :], y_all[:, i, 0, :], ACT.Copy, scale=gates[:, i, 0:1]).then_inc(y_first, 1)
            for i in range(TT):
                act.wait_ge(f_sum, i + 1)
                nc.scalar.activation(fin_junk, fin[:, i, :], ACT.Square, accum_out=stat[:, 0, i:i + 1]).then_inc(f_sq, 1)
                act.wait_ge(f_sq, i + 1)
                root(stat[:, 1, i:i + 1])

        @block.vector
        def _(dve):
            link = linker(dve, dve_chain)
            TS, STT, TTo = nc.vector.tensor_scalar, nc.vector.scalar_tensor_tensor, nc.vector.tensor_tensor
            link(nc.vector.memset(xa_pad[:, :, 0:PADC], 0.0))

            rms_n = [0]

            def rstd(dst, src, link=link):
                rms_n[0] += 1
                TS(dst, src, 1.0 / D, EPS, ALU.mult, ALU.add).then_inc(ms_ok, 1)
                dve.wait_ge(rms_ok, rms_n[0])
                link(nc.vector.reciprocal(dst, dst))

            dve.wait_ge(vecT_ok, 1)
            nc.vector.tensor_copy(cols, bank[7][:, 0:48]).then_inc(cols_ok, 1)
            dve.wait_ge(cols_ok, 1)
            lam = cols[:, COL["lru_lambda"]:COL["lru_lambda"] + FT]
            STT(lru_c[:, 0, :], lam, -1.0, lam, ALU.mult, ALU.max).then_inc(lam_abs_ok, 1)
            dve.wait_ge(c_sig_ok, 1)
            link(TTo(c_sig, c_sig, c_col, ALU.mult))
            nc.vector.tensor_copy(c_rep, c_sig.unsqueeze(2).to_broadcast([P, KT, H])).then_inc(c_ok, 1)
            for i in range(TT):
                dve.wait_ge(x_sq, i + 1)
                rstd(stat[:, 1, i:i + 1], stat[:, 0, i:i + 1])
                TS(xn[:, i, :], x1[:, i, :], stat[:, 1, i:i + 1], None, ALU.mult).then_inc(xn_ok, 1)
            dve.wait_ge(lam_exp_ok, 1)
            z, q, q2, p = lru_c[:, 1, :], lru_c[:, 2, :], lru_c[:, 3, :], lru_c[:, 4, :]
            link(TS(q, z, 2.0, None, ALU.add))
            link(nc.vector.reciprocal(q, q))
            link(TTo(q, q, z, ALU.mult))
            link(TTo(q2, q, q, ALU.mult))
            link(TS(p, q2, 1.0 / 15, None, ALU.mult))
            for d in (13, 11, 9, 7, 5, 3):
                link(STT(p, p, 1.0 / d, q2, ALU.add, ALU.mult))
            link(STT(p, p, 1.0, q, ALU.add, ALU.mult))
            link(TS(q, lam, -1.0, 0.0, ALU.mult, ALU.max))
            link(STT(p, p, 2.0, q, ALU.mult, ALU.add))
            link(TS(lru_c[:, 5, :], p, -LRU_C, None, ALU.mult))
            link(TS(lru_c[:, 6, :], p, -2.0 * LRU_C, None, ALU.mult))
            TS(lru_c[:, 7, :], p, LRU_C, None, ALU.mult).then_inc(lru_c_ok, 1)
            link(TTo(pool_pb, cols[:, COL["pool_b"]:COL["pool_b"] + FT], cols[:, COL["pool_scale"]:COL["pool_scale"] + FT],
                     ALU.mult))
            dve.wait_ge(window_ok, 1)
            nc.vector.reciprocal(inv_count, inv_count).then_inc(pool_const, 1)

            def mod_vector(v):
                row = ada_rows[:, v, :]
                dve.wait_ge(ada_used, (v + 1) * (KT // AK))
                dve.wait_ge(rows_in, 5 * J * 16)
                add = TTo(row, bank[6 + v % 2][:, 0:QW], row, ALU.add)
                gain = {1: 0, 2: 1, 4: 2, 5: 3}.get(v)
                if gain is None:
                    add.then_inc(mod_row, 1)
                    return
                link(add)
                g = gain_rows[:, gain, :]
                if v in (1, 4):
                    STT(row, row, 1.0, g, ALU.add, ALU.mult).then_inc(mod_row, 1)
                else:
                    TTo(row, row, g, ALU.mult).then_inc(mod_row, 1)

            mod_vector(0)
            mod_vector(1)
            dve.wait_ge(mod_colT, 1)
            cT = bank[5][:, :].rearrange("p (v m j r) -> p v m j r", v=2, m=QM, j=J)
            for v in range(2):
                for m in range(QM):
                    last = nc.vector.tensor_copy(mod_col[:, v, :, m], cT[:, v, m, :, 0])
                    if (v, m) == (1, QM - 1):
                        last.then_inc(mod_col_ok, 1)
                    else:
                        link(last)
            for f in range(FT):
                dve.wait_ge(evac, number["xa", f] + 1)
                y = conv_x[:, f, :]
                for k in range(CONV):
                    w = cols[:, k * FT + f:k * FT + f + 1]
                    src = xa_pad[:, f % 2, PADC - k:PADC - k + T]
                    if k == 0:
                        link(TS(y, src, w, col("conv_b", f), ALU.mult, ALU.add))
                    elif k < CONV - 1:
                        link(STT(y, src, w, y, ALU.mult, ALU.add))
                    else:
                        STT(y, src, w, y, ALU.mult, ALU.add).then_inc(conv_ok, 1)
            dve.wait_ge(conv_ok, FT)

            def gelu_end(f):
                dve.wait_ge(gel_sig, f + 1)
                link(TTo(gel, gel, ga[:, f % 2, :], ALU.mult))
                TTo(catT[:, f, :], catT[:, f, :], gel, ALU.mult).then_inc(gel_ok, 1)

            for f in range(FT):
                mod_vector(2 + f)
                dve.wait_ge(lru_in, 3 * f + 3)
                th, b = tanh_m[:, f % 2, :], igate[:, f % 2, :]
                STT(th, decay2[:, f % 2, :], 1.0, th, ALU.add, ALU.mult).then_inc(m2_ok, 1)
                link(TTo(b, b, conv_x[:, f, :], ALU.mult))
                dve.wait_ge(root_ok, f + 1)
                link(TTo(b, b, th, ALU.mult))
                nc.vector.tensor_tensor_scan(catT[:, f, :], decay[:, f % 2, :], b, 0.0, ALU.mult, ALU.add)\
                    .then_inc(lru_ok, 1)
                dve.wait_ge(lru_ok, f + 1)
                if f:
                    gelu_end(f - 1)
                dve.wait_ge(evac, number["ga", f] + 1)
                g = ga[:, f % 2, :]
                if f:
                    dve.wait_ge(gel_ok, f)
                link(TTo(gel, g, g, ALU.mult))
                link(TS(gel, gel, 0.044715, 1.0, ALU.mult, ALU.add))
                TTo(gel, gel, g, ALU.mult).then_inc(gel_in, 1)
            gelu_end(FT - 1)

            for i in range(TT):
                dve.wait_ge(evac, number["mix", i, 1] + 1)
                link(TTo(stat[:, 4, i:i + 1], stat[:, 2, i:i + 1], stat[:, 3, i:i + 1], ALU.add))
                rstd(stat[:, 4, i:i + 1], stat[:, 4, i:i + 1])
                if i == 0:
                    dve.wait_ge(bc_ok, 8)
                m = mixb[:, i % 2, :]
                link(STT(m, m, stat[:, 4, i:i + 1], bc[:, 0, :], ALU.mult, ALU.mult))
                TTo(x1[:, i, :], x1[:, i, :], m, ALU.add).then_inc(x1_ok, 1)
                dve.wait_ge(x1_ok, i + 1)
                dve.wait_ge(x1_sq, i + 1)
                rstd(stat[:, 6, i:i + 1], stat[:, 5, i:i + 1])
                if i >= 2:
                    dve.wait_ge(evac, number["hT", i - 2, 1] + 1)
                    dve.wait_ge(h_stored[i % 2], 16 * (i // 2))
                h = hn[:, i % 2, :]
                link(STT(h, x1[:, i, :], stat[:, 6, i:i + 1], bc[:, 2, :], ALU.mult, ALU.mult))
                TTo(h, h, bc[:, 1, :], ALU.add).then_inc(hn_ok, 1)

            dve.wait_ge(evac, number["logits", TT - 1] + 1)
            dve.wait_ge(router_in, 32)
            dve.wait_ge(route_const, 6)
            dve.wait_ge(hn_ok, TT)

            def over(v, axis, *shape):
                return v.unsqueeze(axis).to_broadcast(list(shape))
            for j in range(J):
                link(nc.vector.memset(j_off[H * j:H * j + H, :], float(j - J)))
            link(TTo(logits, logits, over(router_bias[:, :], 1, P, TT, E), ALU.add))
            for i in range(TT):
                link(nc.vector.max(top[:, i, :], logits[:, i, :]))
                link(nc.vector.max_index(top_i[:, i, :], top[:, i, :], logits[:, i, :]))
            link(nc.vector.tensor_copy(tk_f[:, 0, :].rearrange("p (i k) -> p i k", i=TT), top_i[:, :, 0:TOPK]))
            link(TTo(hot_e.rearrange("p i k e -> p (i k) e"), over(iota_e, 1, P, TK, E), over(tk_f[:, 0, :], 2, P, TK, E),
                     ALU.is_equal))
            link(TTo(sel, hot_e[:, :, 0, :], hot_e[:, :, 1, :], ALU.add))
            link(TTo(sel, sel, hot_e[:, :, 2, :], ALU.add))
            TTo(sel, sel, hot_e[:, :, 3, :], ALU.add).then_inc(sel_ok, 1)
            TTo(top_d, top[:, :, 0:TOPK], top[:, :, 0:1].to_broadcast([P, TT, TOPK]), ALU.subtract).then_inc(top_ok, 1)
            dve.wait_ge(top_exp, 1)
            link(nc.vector.reduce_sum(top_d[:, :, 0], top_e, axis=AX.X))
            link(nc.vector.reciprocal(top_d[:, :, 1], top_d[:, :, 0]))
            link(TTo(gates[:, :, :], top_e, top_d[:, :, 1:2].to_broadcast([P, TT, TOPK]), ALU.mult))
            dve.wait_ge(rank_ok, 1)
            link(TS(exp_i[:, 0, :], bank[5][:, 0:E], float(H - 1), None, ALU.add))
            link(TS(exp_i[:, 1, :], exp_i[:, 0, :], 5, None, ALU.arith_shift_right))
            link(TS(exp_i[:, 0, :], exp_i[:, 1, :], 1, None, ALU.add))
            link(TS(exp_i[:, 2, :], exp_i[:, 0, :], 1, None, ALU.arith_shift_right))
            nc.vector.tensor_copy(counts[0:1, 0, :], exp_i[0:1, 2, :]).then_inc(counts_ok, 1)
            nc.vector.tensor_copy(counts[0:1, 1, :], exp_i[0:1, 1, :]).then_inc(counts_ok, 1)
            link(nc.vector.tensor_copy(exp_f[:, 0, :], exp_i[:, 2, :]))
            link(nc.vector.tensor_tensor_scan(exp_f[:, 1, :], ones[:, 0:E], exp_f[:, 0, :], 0.0, ALU.mult, ALU.add))
            link(TTo(exp_f[:, 2, :], exp_f[:, 1, :], exp_f[:, 0, :], ALU.subtract))
            link(TS(exp_f[:, 3, :], exp_f[:, 2, :], float(2 * H), None, ALU.mult))
            link(TTo(slot_e, bank[4][:, 0:TT * E].rearrange("p (i e) -> p i e", i=TT), over(exp_f[:, 3, :], 1, P, TT, E),
                     ALU.add))
            link(TTo(route_tmp.rearrange("p (i k) e -> p i k e", i=TT), hot_e, over(slot_e, 2, P, TT, TOPK, E), ALU.mult))
            link(nc.vector.reduce_sum(tk_f[:, 1, :], route_tmp, axis=AX.X))
            link(nc.vector.tensor_copy(tk_i[:, 0, :], tk_f[:, 1, :]))
            link(TS(tk_i[:, 1, :], tk_i[:, 0, :], 5, None, ALU.arith_shift_right))
            link(TS(tk_i[:, 2, :], tk_i[:, 0, :], H - 1, None, ALU.bitwise_and))
            link(nc.vector.tensor_copy(tk_f[:, 2:4, :], tk_i[:, 1:3, :]))
            link(TTo(hot_t, over(iota_t, 1, P, TK, P), over(tk_f[:, 3, :], 2, P, TK, P), ALU.is_equal))
            link(TTo(slot_val[:, :, 0, :], over(iota_q, 1, P, TK, NQ), over(tk_f[:, 2, :], 2, P, TK, NQ), ALU.is_equal))
            link(TTo(slot_val[:, :, 1, :], slot_val[:, :, 0, :], over(tok_no[:, 1, :], 2, P, TK, NQ), ALU.mult))
            TTo(slot_val[:, :, 0, :], slot_val[:, :, 0, :], over(tok_no[:, 0, :], 2, P, TK, NQ), ALU.mult)\
                .then_inc(slots_ok, 1)
            dve.wait_ge(table_ok, 1)
            tab = bank[6][:, 0:2 * NQ]
            link(TS(idx_e, tab, 0.0, float(EMPTY), ALU.is_equal, ALU.mult))
            link(TS(idx_f, tab, float(J), j_off, ALU.mult, ALU.add))
            TTo(idx.rearrange("p v s h -> p (v s h)"), idx_f, idx_e, ALU.add).then_inc(idx_ok, 1)
            dve.wait_ge(idx_ok, 1)

            def activate(hf, n, slot, bias_arrived):
                dve.wait_ge(bias_in[slot], bias_arrived)
                dve.wait_ge(u_ps[hf], n + 1)
                u = u_sb[:, hf, :].rearrange("p (n two) -> p n two", two=2)
                TTo(u_sb[:, hf, :], bank[hf][:, :], b1_bc[:, slot, :], ALU.add).then_inc(u_ok[hf], 1)
                dve.wait_ge(u_ok[hf], n + 1)
                TS(glu[:, hf, :], u[:, :, 0], LIMIT, None, ALU.min).then_inc(glu_ok[hf], 1)
                TS(lin[:, hf, :], u[:, :, 1], LIMIT, -LIMIT, ALU.min, ALU.max).then_inc(lin_ok[hf], 1)
                dve.wait_ge(lin_ok[hf], n + 1)
                STT(lin[:, hf, :], lin[:, hf, :], 1.0, glu[:, hf, :], ALU.add, ALU.mult).then_inc(mul_ok[hf], 1)
                dve.wait_ge(mul_ok[hf], n + 1)
                dve.wait_ge(sig_ok[hf], n + 1)
                TTo(glu[:, hf, :], lin[:, hf, :], sig[:, hf, :], ALU.mult).then_inc(act_ok[hf], 1)

            def finish(hf, n, slot):
                dve.wait_ge(y_ps[hf], n + 1)
                dve.wait_ge(y_stored[hf], 16 * n + 16)
                TTo(y_sb[hf], bank[4 + hf][:, 0:QW], b2_bc[:, slot, :], ALU.add).then_inc(y_ok[hf], 1)

            dve.wait_ge(counts_ok, 2)
            step, full = dve.alloc_register("dve_step"), dve.alloc_register("dve_full")
            dve.reg_mov(step, 0)
            dve.reg_mov(full, 0)
            with dve.Fori(0, E // 2) as pair:
                for slot in range(2):
                    e = 2 * pair + slot
                    n_steps = dve.value_load(counts[0:1, 0, bass.ds(e, 1)], min_val=0, max_val=T // (2 * H))
                    n_halves = dve.value_load(counts[0:1, 1, bass.ds(e, 1)], min_val=0, max_val=T // H)
                    bias_arrived = dve.snap(BIAS_INC * pair + BIAS_INC, min_val=BIAS_INC, max_val=BIAS_INC * E)
                    with dve.If(n_steps > 0):
                        with dve.Fori(0, n_steps) as k:
                            s = dve.snap(step, min_val=0, max_val=STEPS_MAX)
                            n = dve.snap(full, min_val=0, max_val=STEPS_MAX)
                            activate(0, s, slot, bias_arrived)
                            with dve.If(2 * k + 1 < n_halves):
                                activate(1, n, slot, bias_arrived)
                            finish(0, s, slot)
                            with dve.If(2 * k + 1 < n_halves):
                                finish(1, n, slot)
                                dve.reg_add(full, full, 1)
                            dve.reg_add(step, step, 1)
                    dve.wait_ge(bias_in[slot], bias_arrived)
                    apart(dve)
                    dve.drain().then_inc(bias_done, 1)

            link2 = linker(dve, f_chain)
            for i in range(TT):
                dve.wait_ge(y_first, i + 1)
                dve.wait_ge(y_in[i], 16)
                f = fin[:, i, :]
                for k in range(1, TOPK):
                    ins = STT(f, y_all[:, i, k, :], gates[:, i, k:k + 1], f, ALU.mult, ALU.add)
                    if k < TOPK - 1:
                        link2(ins)
                    else:
                        ins.then_inc(f_sum, 1)
            for i in range(TT):
                dve.wait_ge(f_sq, i + 1)
                rstd(stat[:, 1, i:i + 1], stat[:, 0, i:i + 1], link2)
                f = fin[:, i, :]
                link2(STT(f, f, stat[:, 1, i:i + 1], gate_f_bc[:, :], ALU.mult, ALU.mult))
                TTo(f, f, x1[:, i, :], ALU.add).then_inc(out_ok, 1)

        @block.tensor
        def _(pe):
            mm, tr = nc.tensor.matmul, nc.tensor.transpose
            pe.wait_ge(ident_ok, 2)
            pe.wait_ge(vec_in, 8 * 16)
            tr(bank[7][:, 0:48], vec_rows[0:48, :], ident[0:48, 0:48]).then_inc(vecT_ok, 1)

            def ready(what):
                n = number[what]
                if n >= R:
                    pe.wait_ge(evac, n - R + 1)
                return bank[n % R]

            def mod(v):
                if v == 1:
                    pe.wait_ge(cols_ok, 1)
                if v >= 2:
                    pe.wait_ge(mod_row, v - 1)
                for kk in range(KT // AK):
                    n = v * (KT // AK) + kk
                    pe.wait_ge(ada_in[n % ADA_RING], 16 * (n // ADA_RING + 1))
                    for k in range(AK):
                        for j in range(J):
                            last = mm(bank[6 + v % 2][H * j:H * j + H, 0:QW], c_rep[:, kk * AK + k, :],
                                      ada_ring[:, n % ADA_RING, k, QW * j:QW * j + QW],
                                      start=(kk == 0 and k == 0), stop=(kk == KT // AK - 1 and k == AK - 1))
                    last.then_inc(ada_used, 1)

            pe.wait_ge(xn_ok, TT)
            for k in range(R):
                ps = ready(("xT", k))
                for i in range(TT):
                    last = tr(ps[:, i * P:(i + 1) * P], xn[:, i, k * P:(k + 1) * P], ident[:, :])
                last.then_inc(prod, 1)
            pe.wait_ge(c_ok, 1)
            mod(0)
            mod(1)
            pe.wait_ge(mod_row, 2)
            for v in range(2):
                for m in range(QM):
                    at = (v * QM + m) * P
                    last = tr(bank[5][:, at:at + P], ada_rows[:, v, m * P:(m + 1) * P], ident[:, :])
            last.then_inc(mod_colT, 1)
            for k in range(R, KT):
                ps = ready(("xT", k))
                for i in range(TT):
                    last = tr(ps[:, i * P:(i + 1) * P], xn[:, i, k * P:(k + 1) * P], ident[:, :])
                last.then_inc(prod, 1)
            pe.wait_ge(evac, KT)

            def u_part(name, slot, count):
                pe.wait_ge(win_in[slot], 16 * count)
                for f in range(FT):
                    ps = ready((name, f))
                    for k in range(KT):
                        last = mm(ps[:, :], win_ring[:, slot, k, f * P:(f + 1) * P], hT[:, k, :], start=(k == 0),
                                  stop=(k == KT - 1))
                    last.then_inc(prod, 1)
                    yield f

            for _ in u_part("xa", 0, 1):
                pass
            for _ in u_part("xb", 1, 1):
                pass
            pe.wait_ge(bd_in, 4 * 16)
            ga_parts = u_part("ga", 0, 2)
            for f in range(FT):
                mod(2 + f)
                pe.wait_ge(conv_ok, f + 1)
                for n, name in enumerate(("r", "i")):
                    ps = ready((name, f))
                    mm(ps[:, :], gate_bd[:, n, f, :], conv_x[:, f, :], start=True, stop=True).then_inc(prod, 1)
                next(ga_parts)
            pe.wait_ge(pool_in, 16)
            for g in range(FT):
                pe.wait_ge(pool_ok, g + 1)
                ps = ready(("pool", g))
                mm(ps[:, :], pool_sb[:, g, :], catT[:, FT + g, :], start=True, stop=True).then_inc(prod, 1)
            pe.wait_ge(wout_in, 16)
            pe.wait_ge(gel_ok, FT)
            pe.wait_ge(evac, number["pool", FT - 1] + 1)
            pe.wait_ge(router_in, 32)
            for what in order[number["mix", 0, 0]:]:
                i = what[1]
                if what[0] == "hT":
                    pe.wait_ge(hn_ok, i + 1)
                if what[0] == "logits":
                    pe.wait_ge(evac, number["hT", i, 1] + 1)
                ps = ready(what)
                if what[0] == "mix":
                    n = what[2]
                    for k in range(KT):
                        last = mm(ps[:, :], catT[:, k, i * P:(i + 1) * P], W2[:, k, n * 512:(n + 1) * 512],
                                  start=(k == 0), stop=(k == KT - 1))
                elif what[0] == "hT":
                    for k in range(HALF):
                        col_at = (what[2] * HALF + k) * P
                        last = tr(ps[:, k * P:(k + 1) * P], hn[:, i % 2, col_at:col_at + P], ident[:, :])
                else:
                    for k in range(KT):
                        last = mm(ps[:, 0:E], h2T[:, i % 2, k, :], router_sb[:, k, :], start=(k == 0), stop=(k == KT - 1))
                last.then_inc(prod, 1)
                if what == ("mix", 0, 1):
                    pe.wait_ge(mod_row, 6)
                    for v in range(4):
                        if v:
                            pe.wait_ge(bc_ok, 2 * v)
                        for j in range(J):
                            last = mm(bank[4 + j // 2][:, (j % 2) * QW:(j % 2 + 1) * QW], ident[:, H * j:H * j + 1].to_broadcast([P, P]),
                                      ada_rows[:, 2 + v, :], start=True, stop=True)
                        last.then_inc(bc_ps, 1)

            pe.wait_ge(route_const, 6)
            pe.wait_ge(sel_ok, 1)
            pe.wait_ge(bc_ok, 8)
            for i in range(TT):
                for b in range(i + 1):
                    mm(bank[4][:, i * E:(i + 1) * E], upper if b == i else ones[:, :], sel[:, b, :], start=(b == 0),
                       stop=(b == i))
            for i in range(TT):
                last = mm(bank[5][:, 0:E], ones[:, :], sel[:, i, :], start=(i == 0), stop=(i == TT - 1))
            last.then_inc(rank_ok, 1)
            pe.wait_ge(slots_ok, 1)
            for n in range(TK):
                last = mm(bank[6][:, 0:2 * NQ], hot_t[:, n, :], slot_val[:, n, :, :].rearrange("p a b -> p (a b)"),
                          start=(n == 0), stop=(n == TK - 1))
            last.then_inc(table_ok, 1)

            def transpose_x(s, first=False):
                pe.wait_ge(xg_in, 32 * s + 32)
                if not first:
                    pe.wait_ge(xT_ok, s)
                for hf in range(2):
                    for m in range(QM):
                        at = (hf * QM + m) * P
                        last = tr(bank[2][:, at:at + P], xg[hf][:, m * P:(m + 1) * P], ident[:, :])
                last.then_inc(xT_ps, 1)

            def up(hf, slot, arrived):
                for k in range(KT):
                    if k % CHUNK == 0:
                        pe.wait_ge(w1_in[slot][k // CHUNK], arrived)
                    for j in range(J):
                        last = mm(bank[hf][H * j:H * j + H, :], xT[:, hf, k % QM, H * (k // QM):H * (k // QM) + H],
                                  W1[:, slot, k, UW * j:UW * j + UW], start=(k == 0), stop=(k == KT - 1))
                last.then_inc(u_ps[hf], 1)

            def transpose_g(hf, n):
                pe.wait_ge(act_ok[hf], n + 1)
                for m in range(QM):
                    last = tr(gT_bank[hf][:, m * P:(m + 1) * P], glu[:, hf, m * P:(m + 1) * P], ident[:, :])
                last.then_inc(gT_ps[hf], 1)

            def down(hf, n, arrived):
                pe.wait_ge(gT_ok[hf], n + 1)
                for k in range(KT):
                    if k % HALF == 0:
                        pe.wait_ge(w2_in[k // HALF], arrived)
                    for j in range(J):
                        last = mm(bank[4 + hf][H * j:H * j + H, 0:QW], gT[:, hf, k % QM, H * (k // QM):H * (k // QM) + H],
                                  W2[:, k, QW * j:QW * j + QW], start=(k == 0), stop=(k == KT - 1))
                last.then_inc(y_ps[hf], 1)

            transpose_x(0, first=True)
            pe.wait_ge(counts_ok, 2)
            step, full = pe.alloc_register("pe_step"), pe.alloc_register("pe_full")
            pe.reg_mov(step, 0)
            pe.reg_mov(full, 0)
            with pe.Fori(0, E // 2) as pair:
                for slot in range(2):
                    e = 2 * pair + slot
                    n_steps = pe.value_load(counts[0:1, 0, bass.ds(e, 1)], min_val=0, max_val=T // (2 * H))
                    n_halves = pe.value_load(counts[0:1, 1, bass.ds(e, 1)], min_val=0, max_val=T // H)
                    w1_arrived = pe.snap(16 * pair + 16, min_val=16, max_val=16 * E)
                    w2_arrived = pe.snap(16 * e + 16, min_val=16, max_val=16 * E)
                    with pe.If(n_steps > 0):
                        with pe.Fori(0, n_steps) as k:
                            s = pe.snap(step, min_val=0, max_val=STEPS_MAX)
                            n = pe.snap(full, min_val=0, max_val=STEPS_MAX)
                            pe.wait_ge(xT_ok, s + 1)
                            up(0, slot, w1_arrived)
                            with pe.If(2 * k + 1 < n_halves):
                                up(1, slot, w1_arrived)
                            transpose_x(s + 1)
                            transpose_g(0, s)
                            down(0, s, w2_arrived)
                            with pe.If(2 * k + 1 < n_halves):
                                transpose_g(1, n)
                                down(1, n, w2_arrived)
                                pe.reg_add(full, full, 1)
                            pe.reg_add(step, step, 1)
                    for ch in range(4):
                        pe.wait_ge(w1_in[slot][ch], w1_arrived)
                    for hf in range(2):
                        pe.wait_ge(w2_in[hf], w2_arrived)
                    apart(pe)
                    pe.drain().then_inc(expert_done, 1)
    return nc


_INS = ["x", "c", "w_ada", "b_ada", "norm_mix_pre", "norm_mix_post", "w_in", "conv_w", "conv_b", "gate_a_w", "gate_a_b",
        "gate_x_w", "gate_x_b", "lru_lambda", "pool_w", "pool_b", "pool_scale", "w_out", "norm_ffn_pre",
        "norm_ffn_post", "router_w", "router_b", "expert_w1", "expert_b1", "expert_w2", "expert_b2"]


def kernel(**inputs):
    import numpy as _np
    import concourse.bacc as _bacc
    from concourse import mybir as _mybir
    from concourse.bass_utils import run_bass_kernel_spmd as _run

    nc = _bacc.Bacc("TRN2", target_bir_lowering=False, num_devices=1)
    arrays, args = {}, []
    for name in _INS:
        a = _np.ascontiguousarray(inputs[name])
        arrays[f"in_{name}"] = a
        args.append(nc.dram_tensor(f"in_{name}", a.shape, _mybir.dt.from_np(a.dtype), kind="ExternalInput").ap())
    out = nc.dram_tensor("out_0", arrays["in_x"].shape, _mybir.dt.float32, kind="ExternalOutput").ap()
    hybrid_layer(nc, *args, out)
    r = _run(nc, [arrays], core_ids=[0])
    return r.results[0]["out_0"]
```

```python
import concourse.bass as bass
from concourse import mybir
from contextlib import ExitStack


def hybrid_layer(nc, x, c, w_ada, b_ada, norm_mix_pre, norm_mix_post, w_in, conv_w, conv_b, gate_a_w, gate_a_b,
                 gate_x_w, gate_x_b, lru_lambda, pool_w, pool_b, pool_scale, w_out, norm_ffn_pre, norm_ffn_post,
                 router_w, router_b, expert_w1, expert_b1, expert_w2, expert_b2, out):
    fp32, i32, u32 = mybir.dt.float32, mybir.dt.int32, mybir.dt.uint32
    ALU, ACT, AX = mybir.AluOpType, mybir.ActivationFunctionType, mybir.AxisListType

    P = 128
    T, D = x.shape[1], x.shape[2]
    TT = T // P
    KT = D // P
    E, F2 = expert_w1.shape[1], expert_w1.shape[3]
    F = F2 // 2
    TOPK = 4
    FT = w_in.shape[2] // P // 3
    CONV = conv_w.shape[1]
    LRU_C, EPS, LIMIT, ALPHA = 8.0, 1e-6, 7.0, 1.702
    J = 4
    H = 32
    QW = D // J
    QM = QW // P
    UW = F2 // J
    N2 = 2
    HW = D // N2
    YP = N2 * H
    STEPS_MAX = T * TOPK // (2 * H) + E
    NQ = 2 * STEPS_MAX + 4
    EMPTY = 1 << 20
    PADC, PADP = CONV - 1, 15

    h_rows = nc.dram_tensor("h_rows", (T * J, QW), fp32).ap()
    y_rows = nc.dram_tensor("y_rows", (T * TOPK * N2, HW), fp32).ap()
    h_store = h_rows.rearrange("(t j) c -> t (j c)", j=J)
    y_load = y_rows.rearrange("(t r) c -> t (r c)", r=TOPK * N2)

    w_ada_v = w_ada[0].rearrange("(k p) n -> p k n", p=P)
    w_in_v = w_in[0].rearrange("(k p) n -> p k n", p=P)
    w_out_v = w_out[0].rearrange("(k p) n -> p k n", p=P)
    w1_v = expert_w1[0].rearrange("e (k p) n -> e p k n", p=P)
    w2_v = expert_w2[0].rearrange("e (k p) n -> e p k n", p=P)

    ctx = ExitStack()
    with ctx:
        def sb(name, shape, dt=fp32):
            return ctx.enter_context(nc.sbuf_tensor(name, shape, dt))

        def sem(name):
            return ctx.enter_context(nc.semaphore(name))

        def sems(name, n):
            return [sem(f"{name}{i}") for i in range(n)]

        W1 = sb("W1", [P, 2, KT, F2])
        W2 = sb("W2", [P, KT, D])
        OV = sb("OV", [P, 6656])
        x1 = sb("x1", [P, TT, D])
        gate_f_bc = sb("gate_f_bc", [P, D])
        ident = sb("ident", [P, P])
        ones = sb("ones", [P, P])
        gates = sb("gates", [P, TT, TOPK])
        counts = sb("counts", [1, 3, E], i32)
        src_cur = sb("src_cur", [P, 2], i32)
        dst_cur = [sb("dst_cur_a", [YP, 1], i32), sb("dst_cur_b", [YP, 1], i32)]
        stat = sb("stat", [P, 8, TT])
        router_bias = sb("router_bias", [P, E])

        def carver(area):
            at = [0]

            def take(*shape):
                n = 1
                for size in shape:
                    n *= size
                v = area[:, at[0]:at[0] + n]
                at[0] += n
                assert at[0] <= area.shape[1], (at[0], area.shape)
                if len(shape) > 1:
                    names = "abcd"[:len(shape)]
                    v = v.rearrange(f"p ({' '.join(names)}) -> p {' '.join(names)}", **dict(zip(names, shape)))
                return v
            return take

        def flat(v):
            return v.rearrange("p a b -> p (a b)")

        HALF = KT // 2
        A_lo, A_hi = flat(W1[:, 0, 0:HALF, :]), flat(W1[:, 0, HALF:KT, :])
        B_lo, B_hi = flat(W1[:, 1, 0:HALF, :]), flat(W1[:, 1, HALF:KT, :])

        ADA_RING, AK = 3, 2
        take = carver(A_lo)
        ada_ring = take(ADA_RING, AK, D)
        gate_bd = take(2, FT, P)
        pool_sb = take(FT, P)
        inv_count = take(PADP + 1)
        mod_col = take(2, J, QM)
        lru_c = take(8, FT)
        pool_pb = take(FT)
        c_sig = take(KT)
        take = carver(A_hi)
        conv_x = take(FT, T)
        rgate = take(T)
        igate = take(2, T)
        decay = take(2, T)
        decay2 = take(2, T)
        tanh_m = take(2, T)
        xa_pad = take(2, T + PADC)
        c_rep = take(KT, H)
        cols = take(48)
        win_ring = carver(B_lo)(2, KT, FT * P)
        take = carver(B_lo)
        mixb = take(2, D)
        junk = take(D)
        hn = take(2, D)
        h2T = take(2, KT, P)
        take = carver(B_hi)
        hT = take(KT, T)
        xb_pad = take(2, T + PADP)
        sums = take(2, T + PADP)
        ga = take(2, T)
        gel = take(T)
        B_HI = B_hi.shape[1]
        router_sb = carver(B_hi[:, B_HI - KT * E:])(KT, E)
        vec_rows = carver(B_hi[:, B_HI - KT * E - P:])(P)
        bc = carver(B_hi[:, KT * T:])(3, D)
        TK = TT * TOPK
        take = carver(B_hi)
        slot_val = take(TK, 2, NQ)
        hot_t = take(TK, P)
        hot_e = take(TT, TOPK, E)
        route_tmp = take(TK, E)
        catT = carver(OV)(KT, T)
        xn = carver(OV)(TT, D)
        take = carver(OV[:, KT * T:])
        ada_rows = take(6, QW)
        gain_rows = take(4, QW)
        take = carver(OV[:, KT * T:])
        iota_q = take(NQ)
        iota_t = take(P)
        iota_e = take(E)
        upper = take(P)
        tok_no = take(2, TK)
        j_off = take(2)
        logits = take(TT, E)
        top = take(TT, 8)
        top_i = take(TT, 8).bitcast(u32)
        sel = take(TT, E)
        slot_e = take(TT, E)
        exp_f = take(4, E)
        exp_i = take(3, E).bitcast(i32)
        tk_f = take(4, TK)
        tk_i = take(3, TK).bitcast(i32)
        top_d = take(TT, TOPK)
        top_e = take(TT, TOPK)
        idx_f = take(2 * NQ)
        idx_e = take(2 * NQ)
        take = carver(OV)
        xg = [take(QW), take(QW)]
        xT = take(2, QM, P)
        b1_bc = take(2, UW)
        b2_and_y1 = take(2, HW)
        b2_bc = b2_and_y1[YP:2 * YP]
        y_part = b2_and_y1[0:YP]
        u_sb = take(2, UW)
        act_g = take(2, QW)
        gT = take(2, QM, P)
        y_sb = [take(HW)[0:YP], take(HW)[0:YP]]
        idx = take(2, NQ // 2, 2).bitcast(i32)
        y_all = carver(flat(W1[:, 0, :, :]))(TT, TOPK, D)
        fin = carver(B_lo)(TT, D)
        fin_junk = carver(B_hi)(D)

        bank = [ctx.enter_context(nc.psum_tensor(f"bank{i}", [P, 512], fp32)) for i in range(8)]
        R = 4

        order = [("xT", k) for k in range(KT)] + [("xa", f) for f in range(FT)] + [("xb", f) for f in range(FT)]
        for f in range(FT):
            order += [("r", f), ("i", f), ("ga", f)]
        order += [("pool", f) for f in range(FT)]
        for i in range(TT):
            order += [("mix", i, 0), ("mix", i, 1)]
            if i >= 1:
                order += [("hT", i - 1, 0), ("hT", i - 1, 1), ("logits", i - 1)]
        order += [("hT", TT - 1, 0), ("hT", TT - 1, 1), ("logits", TT - 1)]
        number = {what: n for n, what in enumerate(order)}

        x_in = sems("x_in", TT)
        vec_in = sem("vec_in")
        ada_in = sems("ada_in", ADA_RING)
        win_in = sems("win_in", 2)
        wout_in = sem("wout_in")
        rows_in = sem("rows_in")
        bd_in = sem("bd_in")
        pool_in = sem("pool_in")
        router_in = sem("router_in")
        window_ok = sem("window_ok")
        pool_const = sem("pool_const")
        ident_ok = sem("ident_ok")
        pads_ok = sem("pads_ok")
        x_sq = sem("x_sq")
        xn_ok = sem("xn_ok")
        vecT_ok = sem("vecT_ok")
        cols_ok = sem("cols_ok")
        c_sig_ok = sem("c_sig_ok")
        c_ok = sem("c_ok")
        lam_abs_ok = sem("lam_abs_ok")
        lam_exp_ok = sem("lam_exp_ok")
        lru_c_ok = sem("lru_c_ok")
        ada_used = sem("ada_used")
        mod_row = sem("mod_row")
        mod_colT = sem("mod_colT")
        mod_col_ok = sem("mod_col_ok")
        prod = sem("prod")
        evac = sem("evac")
        conv_ok = sem("conv_ok")
        pool_ok = sem("pool_ok")
        lru_in = sem("lru_in")
        lru_ok = sem("lru_ok")
        gel_in = sem("gel_in")
        gel_sig = sem("gel_sig")
        gel_ok = sem("gel_ok")
        bc_ps = sem("bc_ps")
        bc_ok = sem("bc_ok")
        x1_ok = sem("x1_ok")
        x1_sq = sem("x1_sq")
        hn_ok = sem("hn_ok")
        h_stored = sems("h_stored", 2)
        route_const = sem("route_const")
        sel_ok = sem("sel_ok")
        rank_ok = sem("rank_ok")
        top_ok = sem("top_ok")
        top_exp = sem("top_exp")
        counts_ok = sem("counts_ok")
        slots_ok = sem("slots_ok")
        table_ok = sem("table_ok")
        idx_ok = sem("idx_ok")
        ms_ok = sem("ms_ok")
        rms_ok = sem("rms_ok")
        m2_ok = sem("m2_ok")
        root_ok = sem("root_ok")
        apart_n = sem("apart_n")
        dve_chain = sem("dve_chain")
        act_chain = sem("act_chain")
        pool_chain = sem("pool_chain")
        w1_in = [sems(f"w1_in{s}_", KT) for s in range(2)]
        w2_in = sems("w2_in", 2)
        bias_in = sems("bias_in", 2)
        xg_in = sem("xg_in")
        xT_ps = sem("xT_ps")
        xT_ok = sem("xT_ok")
        u_ps = sems("u_ps", 2)
        u_ok = sems("u_ok", 2)
        lin_ok = sems("lin_ok", 2)
        glu_ok = sems("glu_ok", 2)
        sig_ok = sems("sig_ok", 2)
        mul_ok = sems("mul_ok", 2)
        act_ok = sems("act_ok", 2)
        gT_ps = sems("gT_ps", 2)
        gT_ok = sems("gT_ok", 2)
        y_ps = sems("y_ps", 2)
        y_part_ok = sems("y_part_ok", 2)
        y_ok = sems("y_ok", 2)
        y_stored = sems("y_stored", 2)
        src_ok = sem("src_ok")
        dst_ok = sems("dst_ok", 2)
        moe_done = sem("moe_done")
        y_in = sems("y_in", TT)
        y_first = sem("y_first")
        f_sum = sem("f_sum")
        f_sq = sem("f_sq")
        out_ok = sem("out_ok")
        out_stored = sem("out_stored")

        f_chain = sem("f_chain")
        COL = {name: CONV * FT + n * FT for n, name in enumerate(
            ("conv_b", "gate_a_b", "gate_x_b", "lru_lambda", "pool_b", "pool_scale", "c"))}
        c_col = cols[:, COL["c"]:COL["c"] + KT]
        gT_bank = [bank[3], bank[6]]
        GELU = 2.0 * (2.0 / 3.141592653589793) ** 0.5

        def u_parts(hf):
            return u_sb[:, hf, :].rearrange("p (n two) -> p n two", two=2)

        def col(name, f):
            return cols[:, COL[name] + f:COL[name] + f + 1]

        def flat3(v):
            return v.rearrange("p a b c -> p (a b c)")

        block = ctx.enter_context(nc.Block())

        def apart(engine):
            engine.sem_inc(apart_n, 1)

        def linker(engine, chain):
            n = [0]

            def link(instruction):
                n[0] += 1
                instruction.then_inc(chain, 1)
                engine.wait_ge(chain, n[0])
            return link

        def load_w1(sp, e, slot, k):
            sp.dma_start(W1[:, slot, k, :], w1_v[bass.ds(e, 1), :, k, :].rearrange("e p n -> p (e n)"))\
                .then_inc(w1_in[slot][k], 16)

        W2_halves = W2[:, :, :].rearrange("p (a k) n -> p a k n", a=2)

        def load_w2(engine, e, experts=w2_v):
            for c in range(2):
                for a in range(2):
                    k = a * HALF + 2 * c
                    src = experts[bass.ds(e, 1), :, k:k + 2, :].rearrange("e p k n -> p (e k) n")
                    engine.dma_start(W2_halves[:, a, 2 * c:2 * c + 2, :], src).then_inc(w2_in[c], 16)

        def load_bias(sp, e, slot):
            for j in range(J):
                sp.dma_start(b1_bc[H * j:H * j + H, slot, :], expert_b1[0, bass.ds(e, 1), UW * j:UW * j + UW]
                             .to_broadcast([H, UW])).then_inc(bias_in[slot], 16)
            for n in range(N2):
                sp.dma_start(b2_bc[H * n:H * n + H, slot, :], expert_b2[0, bass.ds(e, 1), HW * n:HW * n + HW]
                             .to_broadcast([H, HW])).then_inc(bias_in[slot], 16)
        BIAS_INC = (J + N2) * 16

        @block.sync
        def _(sp):
            for i in range(TT):
                sp.dma_start(x1[:, i, :], x[0, i * P:(i + 1) * P, :]).then_inc(x_in[i], 16)

            def load_ada(n):
                v, kk = n // (KT // AK), n % (KT // AK)
                if n >= ADA_RING:
                    sp.wait_ge(ada_used, n - ADA_RING + 1)
                sp.dma_start(ada_ring[:, n % ADA_RING, :, :],
                             w_ada_v[:, kk * AK:(kk + 1) * AK, v * D:(v + 1) * D]).then_inc(ada_in[n % ADA_RING], 16)

            def load_win(part, slot):
                sp.dma_start(win_ring[:, slot, :, :], w_in_v[:, :, part * FT * P:(part + 1) * FT * P])\
                    .then_inc(win_in[slot], 16)

            PIECES = KT // AK
            for n in range(2 * PIECES):
                load_ada(n)
            load_win(0, 0)
            load_win(2, 1)
            for n in range(2 * PIECES, 3 * PIECES):
                load_ada(n)
            sp.wait_ge(prod, number["xa", FT - 1] + 1)
            load_win(1, 0)
            sp.dma_start(W2[:, :, :], w_out_v).then_inc(wout_in, 16)
            for n in range(3 * PIECES, 6 * PIECES):
                load_ada(n)
            sp.wait_ge(evac, number["pool", FT - 1] + 1)
            sp.wait_ge(ada_used, 6 * PIECES)
            sp.wait_ge(lru_ok, FT)
            for k in range(KT):
                load_w1(sp, 0, 0, k)
            sp.wait_ge(prod, number["mix", TT - 1, 1] + 1)
            load_w2(sp, 0)
            sp.wait_ge(idx_ok, 1)
            load_bias(sp, 0, 0)
            load_bias(sp, 1, 1)
            for s in range(2):
                sp.wait_ge(h_stored[s], 16 * TT // 2)
            for k in range(KT):
                if k >= 2:
                    sp.wait_ge(w1_in[1][k - 2], 16)
                load_w1(sp, 1, 1, k)
            sp.wait_ge(counts_ok, 3)
            step, full = sp.alloc_register("sp_step"), sp.alloc_register("sp_full")
            sp.reg_mov(step, 1)
            sp.reg_mov(full, 1)
            with sp.Fori(1, E // 2) as pair:
                for slot in range(2):
                    e = 2 * pair + slot
                    n_steps = sp.value_load(counts[0:1, 0, bass.ds(e - 2, 1)], min_val=0, max_val=T // (2 * H))
                    n_full = sp.value_load(counts[0:1, 2, bass.ds(e - 2, 1)], min_val=0, max_val=T // (2 * H))
                    sp.reg_add(step, step, n_steps)
                    sp.reg_add(full, full, n_full)
                    s = sp.snap(step, min_val=1, max_val=STEPS_MAX + 1)
                    n = sp.snap(full, min_val=1, max_val=STEPS_MAX + 1)
                    sp.wait_ge(u_ps[0], s)
                    sp.wait_ge(u_ps[1], n)
                    apart(sp)
                    landed = sp.snap(16 * pair, min_val=16, max_val=16 * E)
                    biases = sp.snap(BIAS_INC * pair, min_val=BIAS_INC, max_val=BIAS_INC * E)
                    landed_now = sp.snap(16 * pair + 16, min_val=16, max_val=16 * E)
                    for k in range(KT):
                        if k >= 2:
                            sp.wait_ge(w1_in[slot][k - 2], landed_now)
                        elif slot == 1:
                            sp.wait_ge(w1_in[0][KT - 2 + k], landed_now)
                        else:
                            sp.wait_ge(w1_in[1][KT - 2 + k], landed)
                        apart(sp)
                        load_w1(sp, e, slot, k)
                    sp.wait_ge(y_ok[0], s)
                    sp.wait_ge(y_ok[1], n)
                    apart(sp)
                    sp.wait_ge(bias_in[slot], biases)
                    apart(sp)
                    load_bias(sp, e, slot)
            sp.wait_ge(moe_done, 1)
            for i in range(TT):
                sp.dma_start(y_all[:, i, :, :].rearrange("p k d -> p (k d)"), y_load[i * P:(i + 1) * P, :])\
                    .then_inc(y_in[i], 16)
            for i in range(TT):
                sp.wait_ge(out_ok, i + 1)
                sp.dma_start(out[0, i * P:(i + 1) * P, :], fin[:, i, :]).then_inc(out_stored, 16)
            sp.wait_ge(out_stored, 16 * TT)

        @block.gpsimd
        def _(pool):
            link = linker(pool, pool_chain)
            link(nc.gpsimd.memset(ident[:, :], 0.0))
            nc.gpsimd.affine_select(out=ident[:, :], in_=ident[:, :], compare_op=ALU.not_equal, fill=1.0, base=0,
                                    pattern=[[-1, P]], channel_multiplier=1).then_inc(ident_ok, 1)
            nc.gpsimd.memset(ones[:, :], 1.0).then_inc(ident_ok, 1)
            for j in range(J):
                part = slice(H * j, H * j + H)
                src = b_ada[0:1, :].rearrange("a (v q c) -> a q v c", v=6, q=J)[:, j, :, :]
                pool.dma_start(ada_rows[part, :, :], src.to_broadcast([H, 6, QW])).then_inc(rows_in, 16)
                for g, gain in enumerate((norm_mix_pre, norm_mix_post, norm_ffn_pre, norm_ffn_post)):
                    pool.dma_start(gain_rows[part, g, :], gain[0:1, QW * j:QW * j + QW].to_broadcast([H, QW]))\
                        .then_inc(rows_in, 16)
            link(nc.gpsimd.memset(gate_bd[:, :, :, :], 0.0))
            for n, w in enumerate((gate_a_w, gate_x_w)):
                for par in range(2):
                    lo = par * (P // 2)
                    pool.dma_start(gate_bd[lo:lo + P // 2, n, :, lo:lo + P // 2],
                                   w[0].rearrange("(f r) i o -> r i f o", r=2)[par]).then_inc(bd_in, 16)
            pool.dma_start(pool_sb, pool_w[0].rearrange("g c d -> c g d")).then_inc(pool_in, 16)
            pool.dma_start(router_sb, router_w[0].rearrange("(k p) e -> p k e", p=P)).then_inc(router_in, 16)
            pool.dma_start(router_bias[:, :], router_b[0:1, :].to_broadcast([P, E])).then_inc(router_in, 16)
            nc.gpsimd.memset(xb_pad[:, :, 0:PADP], 0.0).then_inc(pads_ok, 1)
            nc.gpsimd.iota(inv_count, [[1, PADP + 1]], base=1, channel_multiplier=0,
                           allow_small_or_imprecise_dtypes=True).then_inc(window_ok, 1)
            pool.wait_ge(pool_const, 1)
            L = T + PADP
            for g in range(FT):
                w = 2 ** (g + 1)
                pool.wait_ge(evac, number["xb", g] + 1)
                cur = xb_pad[:, g % 2, :]
                for level in range(g + 1):
                    s, lo = 2 ** level, 2 ** (level + 1) - 1
                    nxt = sums[:, level % 2, :]
                    link(nc.gpsimd.tensor_tensor(nxt[:, lo:L], cur[:, lo:L], cur[:, lo - s:L - s], ALU.add))
                    cur = nxt
                p_out, xb = catT[:, FT + g, :], xb_pad[:, g % 2, PADP:L]
                link(nc.gpsimd.tensor_scalar(p_out, cur[:, PADP:L], 1.0 / w, None, ALU.mult))
                link(nc.gpsimd.tensor_tensor(p_out[:, 0:w - 1], cur[:, PADP:PADP + w - 1], inv_count[:, 0:w - 1], ALU.mult))
                nc.gpsimd.tensor_tensor(p_out, p_out, xb, ALU.subtract).then_inc(pool_ok, 1)
                pool.wait_ge(pool_ok, g + 1)
            pool.wait_ge(bc_ps, 4)
            IMP = dict(allow_small_or_imprecise_dtypes=True)
            nc.gpsimd.iota(iota_q, [[1, NQ]], base=0, channel_multiplier=0, **IMP).then_inc(route_const, 1)
            nc.gpsimd.iota(iota_t, [[0, J], [1, H]], base=0, channel_multiplier=0, **IMP).then_inc(route_const, 1)
            nc.gpsimd.iota(iota_e, [[1, E]], base=0, channel_multiplier=0, **IMP).then_inc(route_const, 1)
            nc.gpsimd.iota(tok_no[:, 0, :], [[P, TT], [0, TOPK]], base=1, channel_multiplier=1, **IMP)\
                .then_inc(route_const, 1)
            nc.gpsimd.iota(tok_no[:, 1, :], [[P * TOPK, TT], [1, TOPK]], base=1, channel_multiplier=TOPK, **IMP)\
                .then_inc(route_const, 1)
            link(nc.gpsimd.memset(upper, 1.0))
            nc.gpsimd.affine_select(out=upper, in_=upper, compare_op=ALU.is_gt, fill=0.0, base=0,
                                    pattern=[[1, P]], channel_multiplier=-1).then_inc(route_const, 1)
            for i in range(TT):
                pool.wait_ge(hn_ok, i + 1)
                pool.dma_start(h_store[i * P:(i + 1) * P, :], hn[:, i % 2, :]).then_inc(h_stored[i % 2], 16)
            for s in range(2):
                pool.wait_ge(h_stored[s], 16 * TT // 2)
            pool.wait_ge(idx_ok, 1)
            link(nc.gpsimd.memset(xg[0], 0.0))
            link(nc.gpsimd.memset(xg[1], 0.0))

            def gather(step):
                nc.gpsimd.tensor_copy(src_cur[:, :].rearrange("p (a b) -> p a b", a=1), idx[:, 0, bass.ds(step, 1), :])\
                    .then_inc(src_ok, 1)
                pool.wait_ge(src_ok, step + 1)
                apart(pool)
                for hf in range(2):
                    pool.indirect_dma_start(xg[hf], None, h_rows, bass.IndirectOffsetOnAxis(ap=src_cur[:, hf:hf + 1], axis=0),
                                            bounds_check=T * J - 1, oob_is_err=False).then_inc(xg_in, 16)

            def scatter(hf, n, step):
                pool.wait_ge(y_ok[hf], n + 1)
                nc.gpsimd.tensor_copy(dst_cur[hf][:, :].rearrange("p (a b) -> p a b", a=1),
                                      idx[0:YP, 1, bass.ds(step, 1), hf:hf + 1]).then_inc(dst_ok[hf], 1)
                pool.wait_ge(dst_ok[hf], n + 1)
                apart(pool)
                pool.indirect_dma_start(y_rows, bass.IndirectOffsetOnAxis(ap=dst_cur[hf][:, 0:1], axis=0), y_sb[hf], None,
                                        bounds_check=T * TOPK * N2 - 1, oob_is_err=False).then_inc(y_stored[hf], 16)

            NOTHING = NQ // 2 - 1
            for hf in range(2):
                nc.gpsimd.memset(y_sb[hf], 0.0).then_inc(y_ok[hf], 1)
            scatter(1, 0, NOTHING)
            gather(0)
            step, full = pool.alloc_register("pool_step"), pool.alloc_register("pool_full")
            before, before_halves = pool.alloc_register("pool_before"), pool.alloc_register("pool_before_halves")
            pool.reg_mov(step, 0)
            pool.reg_mov(full, 0)
            pool.reg_mov(before, NOTHING)
            pool.reg_mov(before_halves, 0)

            def scatter_before():
                s = pool.snap(step, min_val=0, max_val=STEPS_MAX)
                at = pool.snap(before, min_val=0, max_val=NOTHING)
                scatter(0, s, at)
                with pool.If(pool.snap(before_halves, min_val=0, max_val=T // H) > 1):
                    n = pool.snap(full, min_val=0, max_val=STEPS_MAX)
                    at = pool.snap(before, min_val=0, max_val=NOTHING)
                    scatter(1, n + 1, at)
                    pool.reg_add(full, full, 1)

            with pool.Fori(0, E) as e:
                n_steps = pool.value_load(counts[0:1, 0, bass.ds(e, 1)], min_val=0, max_val=T // (2 * H))
                n_halves = pool.value_load(counts[0:1, 1, bass.ds(e, 1)], min_val=0, max_val=T // H)
                with pool.If(n_steps > 0):
                    with pool.Fori(0, n_steps) as k:
                        s = pool.snap(step, min_val=0, max_val=STEPS_MAX)
                        pool.wait_ge(xT_ps, s + 1)
                        apart(pool)
                        gather(s + 1)
                        scatter_before()
                        pool.reg_mov(before, step)
                        pool.reg_mov(before_halves, n_halves - 2 * k)
                        pool.reg_add(step, step, 1)
                pool.nop()
            scatter_before()
            s = pool.snap(step, min_val=0, max_val=STEPS_MAX)
            n = pool.snap(full, min_val=0, max_val=STEPS_MAX)
            pool.wait_ge(y_stored[0], 16 * s + 16)
            pool.wait_ge(y_stored[1], 16 * n + 16)
            apart(pool)
            pool.drain().then_inc(moe_done, 1)

        @block.scalar
        def _(act):
            link = linker(act, act_chain)
            vecs = [(0, conv_w[0].rearrange("k (f p) -> (k f) p", p=P))]
            at = CONV * FT
            for v in (conv_b, gate_a_b, gate_x_b, lru_lambda, pool_b, pool_scale):
                vecs.append((at, v[0].rearrange("(f p) -> f p", p=P)))
                at += FT
            vecs.append((at, c[0].rearrange("(k p) -> k p", p=P)))
            for at, v in vecs:
                act.dma_start(vec_rows[at:at + v.shape[0], :], v).then_inc(vec_in, 16)
            act.wait_ge(cols_ok, 1)
            nc.scalar.activation(c_sig, c_col, ACT.Sigmoid).then_inc(c_sig_ok, 1)
            act.wait_ge(lam_abs_ok, 1)
            nc.scalar.activation(lru_c[:, 1, :], lru_c[:, 0, :], ACT.Exp, scale=-1.0).then_inc(lam_exp_ok, 1)
            for i in range(TT):
                act.wait_ge(x_in[i], 16)
                nc.scalar.activation(hT[:, 2 * i:2 * i + 2, :].rearrange("p a b -> p (a b)"), x1[:, i, :], ACT.Square,
                                     accum_out=stat[:, 0, i:i + 1]).then_inc(x_sq, 1)
            roots = [0]

            def root(v):
                roots[0] += 1
                act.wait_ge(ms_ok, roots[0])
                nc.scalar.activation(v, v, ACT.Sqrt).then_inc(rms_ok, 1)

            for i in range(TT):
                root(stat[:, 1, i:i + 1])

            def take_out(what):
                n = number[what]
                act.wait_ge(prod, n + 1)
                return bank[n % R]

            act.wait_ge(mod_col_ok, 1)
            act.wait_ge(x_sq, TT)
            for k in range(KT):
                ps = take_out(("xT", k))
                nc.scalar.activation(hT[:, k, :], ps[:, :], ACT.Identity, bias=mod_col[:, 0, k // QM, k % QM:k % QM + 1],
                                     scale=mod_col[:, 1, k // QM, k % QM:k % QM + 1]).then_inc(evac, 1)
            for f in range(FT):
                ps = take_out(("xa", f))
                if f >= 2:
                    act.wait_ge(conv_ok, f - 1)
                nc.scalar.activation(xa_pad[:, f % 2, PADC:], ps[:, :], ACT.Copy).then_inc(evac, 1)
            act.wait_ge(pads_ok, 1)
            for f in range(FT):
                ps = take_out(("xb", f))
                if f >= 2:
                    act.wait_ge(pool_ok, f - 1)
                nc.scalar.activation(xb_pad[:, f % 2, PADP:], ps[:, :], ACT.Copy).then_inc(evac, 1)
            act.wait_ge(lru_c_ok, 1)
            for f in range(FT):
                ps = take_out(("r", f))
                if f:
                    act.wait_ge(lru_in, 3 * f)
                nc.scalar.activation(rgate, ps[:, :], ACT.Sigmoid, bias=col("gate_a_b", f)).then_inc(evac, 1)
                ps = take_out(("i", f))
                if f >= 2:
                    act.wait_ge(lru_ok, f - 1)
                nc.scalar.activation(igate[:, f % 2, :], ps[:, :], ACT.Sigmoid, bias=col("gate_x_b", f)).then_inc(evac, 1)
                act.wait_ge(evac, number["i", f] + 1)
                nc.scalar.activation(decay[:, f % 2, :], rgate, ACT.Exp, scale=lru_c[:, 5, f:f + 1]).then_inc(lru_in, 1)
                nc.scalar.activation(decay2[:, f % 2, :], rgate, ACT.Exp, scale=lru_c[:, 6, f:f + 1]).then_inc(lru_in, 1)
                nc.scalar.activation(tanh_m[:, f % 2, :], rgate, ACT.Tanh, scale=lru_c[:, 7, f:f + 1]).then_inc(lru_in, 1)
                act.wait_ge(m2_ok, f + 1)
                nc.scalar.activation(tanh_m[:, f % 2, :], tanh_m[:, f % 2, :], ACT.Sqrt).then_inc(root_ok, 1)
                ps = take_out(("ga", f))
                if f >= 2:
                    act.wait_ge(gel_ok, f - 1)
                nc.scalar.activation(ga[:, f % 2, :], ps[:, :], ACT.Copy).then_inc(evac, 1)
                if f >= 1:
                    act.wait_ge(gel_in, f)
                    nc.scalar.activation(gel, gel, ACT.Sigmoid, scale=GELU).then_inc(gel_sig, 1)
            act.wait_ge(gel_in, FT)
            nc.scalar.activation(gel, gel, ACT.Sigmoid, scale=GELU).then_inc(gel_sig, 1)
            for f in range(FT):
                ps = take_out(("pool", f))
                nc.scalar.activation(catT[:, FT + f, :], ps[:, :], ACT.Identity, bias=pool_pb[:, f:f + 1],
                                     scale=col("pool_scale", f)).then_inc(evac, 1)

            bc_to = [bc[:, 0, :], bc[:, 1, :], bc[:, 2, :], gate_f_bc[:, :]]
            mixes = 0
            for what in order[number["mix", 0, 0]:]:
                ps = take_out(what)
                i = what[1]
                if what[0] == "mix":
                    n = what[2]
                    if i >= 2:
                        act.wait_ge(x1_ok, i - 1)
                    link(nc.scalar.activation(junk[:, 0:512], ps[:, :], ACT.Square, accum_out=stat[:, 2 + n, i:i + 1]))
                    nc.scalar.activation(mixb[:, i % 2, n * 512:(n + 1) * 512], ps[:, :], ACT.Copy).then_inc(evac, 1)
                    if n == 1:
                        if i == 0:
                            for v in range(4):
                                act.wait_ge(bc_ps, v + 1)
                                nc.scalar.activation(bc_to[v][:, 0:512], bank[4][:, :], ACT.Copy).then_inc(bc_ok, 1)
                                nc.scalar.activation(bc_to[v][:, 512:D], bank[5][:, :], ACT.Copy).then_inc(bc_ok, 1)
                        root(stat[:, 4, i:i + 1])
                        act.wait_ge(x1_ok, i + 1)
                        nc.scalar.activation(junk, x1[:, i, :], ACT.Square, accum_out=stat[:, 5, i:i + 1])\
                            .then_inc(x1_sq, 1)
                        act.wait_ge(x1_sq, i + 1)
                        root(stat[:, 6, i:i + 1])
                elif what[0] == "hT":
                    n = what[2]
                    nc.scalar.activation(h2T[:, i % 2, n * HALF:(n + 1) * HALF, :].rearrange("p a b -> p (a b)"), ps[:, :],
                                         ACT.Copy).then_inc(evac, 1)
                else:
                    nc.scalar.activation(logits[:, i, :], ps[:, 0:E], ACT.Copy).then_inc(evac, 1)
            act.wait_ge(top_ok, 1)
            nc.scalar.activation(top_e, top_d, ACT.Exp).then_inc(top_exp, 1)

            act.preload_act_table(ACT.Sigmoid)

            def take_xT(s):
                act.wait_ge(xT_ps, s + 1)
                nc.scalar.activation(flat3(xT), bank[2][:, :], ACT.Copy).then_inc(xT_ok, 1)

            def sigmoid(hf, n):
                act.wait_ge(glu_ok[hf], n + 1)
                nc.scalar.activation(act_g[:, hf, :], u_parts(hf)[:, :, 0], ACT.Sigmoid, scale=ALPHA).then_inc(sig_ok[hf], 1)

            def take_gT(hf, n):
                act.wait_ge(gT_ps[hf], n + 1)
                nc.scalar.activation(flat(gT[:, hf, :, :]), gT_bank[hf][:, 0:QW], ACT.Copy).then_inc(gT_ok[hf], 1)

            take_xT(0)
            act.wait_ge(counts_ok, 3)
            step, full = act.alloc_register("act_step"), act.alloc_register("act_full")
            act.reg_mov(step, 0)
            act.reg_mov(full, 0)

            def expert(e):
                n_steps = act.value_load(counts[0:1, 0, bass.ds(e, 1)], min_val=0, max_val=T // (2 * H))
                n_halves = act.value_load(counts[0:1, 1, bass.ds(e, 1)], min_val=0, max_val=T // H)
                with act.If(n_steps > 0):
                    with act.Fori(0, n_steps) as k:
                        s = act.snap(step, min_val=0, max_val=STEPS_MAX)
                        n = act.snap(full, min_val=0, max_val=STEPS_MAX)
                        sigmoid(0, s)
                        with act.If(2 * k + 1 < n_halves):
                            sigmoid(1, n)
                        take_gT(0, s)
                        take_xT(s + 1)
                        with act.If(2 * k + 1 < n_halves):
                            take_gT(1, n)
                            act.reg_add(full, full, 1)
                        act.reg_add(step, step, 1)
                act.nop()

            with act.Fori(0, E - 1) as e:
                expert(e)
                s = act.snap(step, min_val=0, max_val=STEPS_MAX)
                n = act.snap(full, min_val=0, max_val=STEPS_MAX)
                act.wait_ge(y_ps[0], s + 1)
                apart(act)
                act.wait_ge(y_ps[1], n + 1)
                apart(act)
                for piece in range(2):
                    act.wait_ge(w2_in[piece], 32 * e + 32)
                    apart(act)
                load_w2(act, e, w2_v[1:E])
            expert(E - 1)

            for i in range(TT):
                act.wait_ge(y_in[i], 16)
                nc.scalar.activation(fin[:, i, :], y_all[:, i, 0, :], ACT.Copy, scale=gates[:, i, 0:1]).then_inc(y_first, 1)
            for i in range(TT):
                act.wait_ge(f_sum, i + 1)
                nc.scalar.activation(fin_junk, fin[:, i, :], ACT.Square, accum_out=stat[:, 0, i:i + 1]).then_inc(f_sq, 1)
                act.wait_ge(f_sq, i + 1)
                root(stat[:, 1, i:i + 1])

        @block.vector
        def _(dve):
            link = linker(dve, dve_chain)
            TS, STT, TTo = nc.vector.tensor_scalar, nc.vector.scalar_tensor_tensor, nc.vector.tensor_tensor
            link(nc.vector.memset(xa_pad[:, :, 0:PADC], 0.0))

            rms_n = [0]

            def rstd(dst, src, link=link):
                rms_n[0] += 1
                TS(dst, src, 1.0 / D, EPS, ALU.mult, ALU.add).then_inc(ms_ok, 1)
                dve.wait_ge(rms_ok, rms_n[0])
                link(nc.vector.reciprocal(dst, dst))

            dve.wait_ge(vecT_ok, 1)
            nc.vector.tensor_copy(cols, bank[7][:, 0:48]).then_inc(cols_ok, 1)
            dve.wait_ge(cols_ok, 1)
            lam = cols[:, COL["lru_lambda"]:COL["lru_lambda"] + FT]
            STT(lru_c[:, 0, :], lam, -1.0, lam, ALU.mult, ALU.max).then_inc(lam_abs_ok, 1)
            dve.wait_ge(c_sig_ok, 1)
            link(TTo(c_sig, c_sig, c_col, ALU.mult))
            nc.vector.tensor_copy(c_rep, c_sig.unsqueeze(2).to_broadcast([P, KT, H])).then_inc(c_ok, 1)
            for i in range(TT):
                dve.wait_ge(x_sq, i + 1)
                rstd(stat[:, 1, i:i + 1], stat[:, 0, i:i + 1])
                TS(xn[:, i, :], x1[:, i, :], stat[:, 1, i:i + 1], None, ALU.mult).then_inc(xn_ok, 1)
            dve.wait_ge(lam_exp_ok, 1)
            z, q, q2, p = lru_c[:, 1, :], lru_c[:, 2, :], lru_c[:, 3, :], lru_c[:, 4, :]
            link(TS(q, z, 2.0, None, ALU.add))
            link(nc.vector.reciprocal(q, q))
            link(TTo(q, q, z, ALU.mult))
            link(TTo(q2, q, q, ALU.mult))
            link(TS(p, q2, 1.0 / 15, None, ALU.mult))
            for d in (13, 11, 9, 7, 5, 3):
                link(STT(p, p, 1.0 / d, q2, ALU.add, ALU.mult))
            link(STT(p, p, 1.0, q, ALU.add, ALU.mult))
            link(TS(q, lam, -1.0, 0.0, ALU.mult, ALU.max))
            link(STT(p, p, 2.0, q, ALU.mult, ALU.add))
            link(TS(lru_c[:, 5, :], p, -LRU_C, None, ALU.mult))
            link(TS(lru_c[:, 6, :], p, -2.0 * LRU_C, None, ALU.mult))
            TS(lru_c[:, 7, :], p, LRU_C, None, ALU.mult).then_inc(lru_c_ok, 1)
            link(TTo(pool_pb, cols[:, COL["pool_b"]:COL["pool_b"] + FT], cols[:, COL["pool_scale"]:COL["pool_scale"] + FT],
                     ALU.mult))
            dve.wait_ge(window_ok, 1)
            nc.vector.reciprocal(inv_count, inv_count).then_inc(pool_const, 1)

            def mod_vector(v):
                row = ada_rows[:, v, :]
                dve.wait_ge(ada_used, (v + 1) * (KT // AK))
                dve.wait_ge(rows_in, 5 * J * 16)
                add = TTo(row, bank[6 + v % 2][:, 0:QW], row, ALU.add)
                gain = {1: 0, 2: 1, 4: 2, 5: 3}.get(v)
                if gain is None:
                    add.then_inc(mod_row, 1)
                    return
                link(add)
                g = gain_rows[:, gain, :]
                if v in (1, 4):
                    STT(row, row, 1.0, g, ALU.add, ALU.mult).then_inc(mod_row, 1)
                else:
                    TTo(row, row, g, ALU.mult).then_inc(mod_row, 1)

            mod_vector(0)
            mod_vector(1)
            dve.wait_ge(mod_colT, 1)
            cT = bank[5][:, :].rearrange("p (v m j r) -> p v m j r", v=2, m=QM, j=J)
            for v in range(2):
                for m in range(QM):
                    last = nc.vector.tensor_copy(mod_col[:, v, :, m], cT[:, v, m, :, 0])
                    if (v, m) == (1, QM - 1):
                        last.then_inc(mod_col_ok, 1)
                    else:
                        link(last)
            for f in range(FT):
                dve.wait_ge(evac, number["xa", f] + 1)
                y = conv_x[:, f, :]
                for k in range(CONV):
                    w = cols[:, k * FT + f:k * FT + f + 1]
                    src = xa_pad[:, f % 2, PADC - k:PADC - k + T]
                    if k == 0:
                        link(TS(y, src, w, col("conv_b", f), ALU.mult, ALU.add))
                    elif k < CONV - 1:
                        link(STT(y, src, w, y, ALU.mult, ALU.add))
                    else:
                        STT(y, src, w, y, ALU.mult, ALU.add).then_inc(conv_ok, 1)
            dve.wait_ge(conv_ok, FT)

            def gelu_end(f):
                dve.wait_ge(gel_sig, f + 1)
                link(TTo(gel, gel, ga[:, f % 2, :], ALU.mult))
                TTo(catT[:, f, :], catT[:, f, :], gel, ALU.mult).then_inc(gel_ok, 1)

            for f in range(FT):
                mod_vector(2 + f)
                dve.wait_ge(lru_in, 3 * f + 3)
                th, b = tanh_m[:, f % 2, :], igate[:, f % 2, :]
                STT(th, decay2[:, f % 2, :], 1.0, th, ALU.add, ALU.mult).then_inc(m2_ok, 1)
                link(TTo(b, b, conv_x[:, f, :], ALU.mult))
                dve.wait_ge(root_ok, f + 1)
                link(TTo(b, b, th, ALU.mult))
                nc.vector.tensor_tensor_scan(catT[:, f, :], decay[:, f % 2, :], b, 0.0, ALU.mult, ALU.add)\
                    .then_inc(lru_ok, 1)
                dve.wait_ge(lru_ok, f + 1)
                if f:
                    gelu_end(f - 1)
                dve.wait_ge(evac, number["ga", f] + 1)
                g = ga[:, f % 2, :]
                if f:
                    dve.wait_ge(gel_ok, f)
                link(TTo(gel, g, g, ALU.mult))
                link(TS(gel, gel, 0.044715, 1.0, ALU.mult, ALU.add))
                TTo(gel, gel, g, ALU.mult).then_inc(gel_in, 1)
            gelu_end(FT - 1)

            for i in range(TT):
                dve.wait_ge(evac, number["mix", i, 1] + 1)
                link(TTo(stat[:, 4, i:i + 1], stat[:, 2, i:i + 1], stat[:, 3, i:i + 1], ALU.add))
                rstd(stat[:, 4, i:i + 1], stat[:, 4, i:i + 1])
                if i == 0:
                    dve.wait_ge(bc_ok, 8)
                m = mixb[:, i % 2, :]
                link(STT(m, m, stat[:, 4, i:i + 1], bc[:, 0, :], ALU.mult, ALU.mult))
                TTo(x1[:, i, :], x1[:, i, :], m, ALU.add).then_inc(x1_ok, 1)
                dve.wait_ge(x1_ok, i + 1)
                dve.wait_ge(x1_sq, i + 1)
                rstd(stat[:, 6, i:i + 1], stat[:, 5, i:i + 1])
                if i >= 2:
                    dve.wait_ge(evac, number["hT", i - 2, 1] + 1)
                    dve.wait_ge(h_stored[i % 2], 16 * (i // 2))
                h = hn[:, i % 2, :]
                link(STT(h, x1[:, i, :], stat[:, 6, i:i + 1], bc[:, 2, :], ALU.mult, ALU.mult))
                TTo(h, h, bc[:, 1, :], ALU.add).then_inc(hn_ok, 1)

            dve.wait_ge(evac, number["logits", TT - 1] + 1)
            dve.wait_ge(router_in, 32)
            dve.wait_ge(route_const, 6)
            dve.wait_ge(hn_ok, TT)

            def over(v, axis, *shape):
                return v.unsqueeze(axis).to_broadcast(list(shape))
            for j in range(J):
                link(nc.vector.memset(j_off[H * j:H * j + H, 0:1], float(j - J)))
                link(nc.vector.memset(j_off[H * j:H * j + H, 1:2], float(j - N2)))
            link(TTo(logits, logits, over(router_bias[:, :], 1, P, TT, E), ALU.add))
            for i in range(TT):
                link(nc.vector.max(top[:, i, :], logits[:, i, :]))
                link(nc.vector.max_index(top_i[:, i, :], top[:, i, :], logits[:, i, :]))
            link(nc.vector.tensor_copy(tk_f[:, 0, :].rearrange("p (i k) -> p i k", i=TT), top_i[:, :, 0:TOPK]))
            link(TTo(hot_e.rearrange("p i k e -> p (i k) e"), over(iota_e, 1, P, TK, E), over(tk_f[:, 0, :], 2, P, TK, E),
                     ALU.is_equal))
            link(TTo(sel, hot_e[:, :, 0, :], hot_e[:, :, 1, :], ALU.add))
            link(TTo(sel, sel, hot_e[:, :, 2, :], ALU.add))
            TTo(sel, sel, hot_e[:, :, 3, :], ALU.add).then_inc(sel_ok, 1)
            TTo(top_d, top[:, :, 0:TOPK], top[:, :, 0:1].to_broadcast([P, TT, TOPK]), ALU.subtract).then_inc(top_ok, 1)
            dve.wait_ge(top_exp, 1)
            link(nc.vector.reduce_sum(top_d[:, :, 0], top_e, axis=AX.X))
            link(nc.vector.reciprocal(top_d[:, :, 1], top_d[:, :, 0]))
            link(TTo(gates[:, :, :], top_e, top_d[:, :, 1:2].to_broadcast([P, TT, TOPK]), ALU.mult))
            dve.wait_ge(rank_ok, 1)
            link(TS(exp_i[:, 0, :], bank[5][:, 0:E], float(H - 1), None, ALU.add))
            link(TS(exp_i[:, 1, :], exp_i[:, 0, :], 5, None, ALU.arith_shift_right))
            link(TS(exp_i[:, 0, :], exp_i[:, 1, :], 1, None, ALU.add))
            link(TS(exp_i[:, 2, :], exp_i[:, 0, :], 1, None, ALU.arith_shift_right))
            link(TS(exp_i[:, 0, :], exp_i[:, 1, :], 1, None, ALU.arith_shift_right))
            nc.vector.tensor_copy(counts[0:1, 0, :], exp_i[0:1, 2, :]).then_inc(counts_ok, 1)
            nc.vector.tensor_copy(counts[0:1, 1, :], exp_i[0:1, 1, :]).then_inc(counts_ok, 1)
            nc.vector.tensor_copy(counts[0:1, 2, :], exp_i[0:1, 0, :]).then_inc(counts_ok, 1)
            link(nc.vector.tensor_copy(exp_f[:, 0, :], exp_i[:, 2, :]))
            link(nc.vector.tensor_tensor_scan(exp_f[:, 1, :], ones[:, 0:E], exp_f[:, 0, :], 0.0, ALU.mult, ALU.add))
            link(TTo(exp_f[:, 2, :], exp_f[:, 1, :], exp_f[:, 0, :], ALU.subtract))
            link(TS(exp_f[:, 3, :], exp_f[:, 2, :], float(2 * H), None, ALU.mult))
            link(TTo(slot_e, bank[4][:, 0:TT * E].rearrange("p (i e) -> p i e", i=TT), over(exp_f[:, 3, :], 1, P, TT, E),
                     ALU.add))
            link(TTo(route_tmp.rearrange("p (i k) e -> p i k e", i=TT), hot_e, over(slot_e, 2, P, TT, TOPK, E), ALU.mult))
            link(nc.vector.reduce_sum(tk_f[:, 1, :], route_tmp, axis=AX.X))
            link(nc.vector.tensor_copy(tk_i[:, 0, :], tk_f[:, 1, :]))
            link(TS(tk_i[:, 1, :], tk_i[:, 0, :], 5, None, ALU.arith_shift_right))
            link(TS(tk_i[:, 2, :], tk_i[:, 0, :], H - 1, None, ALU.bitwise_and))
            link(nc.vector.tensor_copy(tk_f[:, 2:4, :], tk_i[:, 1:3, :]))
            link(TTo(hot_t, over(iota_t, 1, P, TK, P), over(tk_f[:, 3, :], 2, P, TK, P), ALU.is_equal))
            link(TTo(slot_val[:, :, 0, :], over(iota_q, 1, P, TK, NQ), over(tk_f[:, 2, :], 2, P, TK, NQ), ALU.is_equal))
            link(TTo(slot_val[:, :, 1, :], slot_val[:, :, 0, :], over(tok_no[:, 1, :], 2, P, TK, NQ), ALU.mult))
            TTo(slot_val[:, :, 0, :], slot_val[:, :, 0, :], over(tok_no[:, 0, :], 2, P, TK, NQ), ALU.mult)\
                .then_inc(slots_ok, 1)
            dve.wait_ge(table_ok, 1)
            tab = bank[6][:, 0:2 * NQ]
            link(TS(idx_e, tab, 0.0, float(EMPTY), ALU.is_equal, ALU.mult))
            link(TS(idx_f[:, 0:NQ], tab[:, 0:NQ], float(J), j_off[:, 0:1], ALU.mult, ALU.add))
            link(TS(idx_f[:, NQ:2 * NQ], tab[:, NQ:2 * NQ], float(N2), j_off[:, 1:2], ALU.mult, ALU.add))
            TTo(idx.rearrange("p v s h -> p (v s h)"), idx_f, idx_e, ALU.add).then_inc(idx_ok, 1)
            dve.wait_ge(idx_ok, 1)

            def activate(hf, n, slot, bias_arrived):
                dve.wait_ge(bias_in[slot], bias_arrived)
                dve.wait_ge(u_ps[hf], n + 2)
                gate, lin = u_parts(hf)[:, :, 0], u_parts(hf)[:, :, 1]
                TTo(u_sb[:, hf, :], bank[hf][:, :], b1_bc[:, slot, :], ALU.add).then_inc(u_ok[hf], 1)
                dve.wait_ge(u_ok[hf], n + 1)
                TS(gate, gate, LIMIT, None, ALU.min).then_inc(glu_ok[hf], 1)
                TS(lin, lin, LIMIT, -LIMIT, ALU.min, ALU.max).then_inc(lin_ok[hf], 1)
                dve.wait_ge(lin_ok[hf], n + 1)
                STT(lin, lin, 1.0, gate, ALU.add, ALU.mult).then_inc(mul_ok[hf], 1)
                dve.wait_ge(mul_ok[hf], n + 1)
                dve.wait_ge(sig_ok[hf], n + 1)
                TTo(act_g[:, hf, :], lin, act_g[:, hf, :], ALU.mult).then_inc(act_ok[hf], 1)

            def finish(hf, n, slot):
                dve.wait_ge(y_ps[hf], n + 2)
                TTo(y_part[:, hf, :], bank[4 + hf][YP:2 * YP, :], b2_bc[:, slot, :], ALU.add).then_inc(y_part_ok[hf], 1)
                dve.wait_ge(y_part_ok[hf], n + 1)
                dve.wait_ge(y_stored[hf], 16 * n + 16)
                TTo(y_sb[hf], bank[4 + hf][0:YP, :], y_part[:, hf, :], ALU.add).then_inc(y_ok[hf], 1)

            dve.wait_ge(counts_ok, 3)
            step, full = dve.alloc_register("dve_step"), dve.alloc_register("dve_full")
            dve.reg_mov(step, 0)
            dve.reg_mov(full, 0)
            with dve.Fori(0, E // 2) as pair:
                for slot in range(2):
                    e = 2 * pair + slot
                    n_steps = dve.value_load(counts[0:1, 0, bass.ds(e, 1)], min_val=0, max_val=T // (2 * H))
                    n_halves = dve.value_load(counts[0:1, 1, bass.ds(e, 1)], min_val=0, max_val=T // H)
                    bias_arrived = dve.snap(BIAS_INC * pair + BIAS_INC, min_val=BIAS_INC, max_val=BIAS_INC * E)
                    with dve.If(n_steps > 0):
                        with dve.Fori(0, n_steps) as k:
                            s = dve.snap(step, min_val=0, max_val=STEPS_MAX)
                            n = dve.snap(full, min_val=0, max_val=STEPS_MAX)
                            activate(0, s, slot, bias_arrived)
                            with dve.If(2 * k + 1 < n_halves):
                                activate(1, n, slot, bias_arrived)
                            finish(0, s, slot)
                            with dve.If(2 * k + 1 < n_halves):
                                finish(1, n, slot)
                                dve.reg_add(full, full, 1)
                            dve.reg_add(step, step, 1)
                dve.nop()

            link2 = linker(dve, f_chain)
            for i in range(TT):
                dve.wait_ge(y_first, i + 1)
                dve.wait_ge(y_in[i], 16)
                f = fin[:, i, :]
                for k in range(1, TOPK):
                    ins = STT(f, y_all[:, i, k, :], gates[:, i, k:k + 1], f, ALU.mult, ALU.add)
                    if k < TOPK - 1:
                        link2(ins)
                    else:
                        ins.then_inc(f_sum, 1)
            for i in range(TT):
                dve.wait_ge(f_sq, i + 1)
                rstd(stat[:, 1, i:i + 1], stat[:, 0, i:i + 1], link2)
                f = fin[:, i, :]
                link2(STT(f, f, stat[:, 1, i:i + 1], gate_f_bc[:, :], ALU.mult, ALU.mult))
                TTo(f, f, x1[:, i, :], ALU.add).then_inc(out_ok, 1)

        @block.tensor
        def _(pe):
            mm, tr = nc.tensor.matmul, nc.tensor.transpose
            pe.wait_ge(ident_ok, 2)
            pe.wait_ge(vec_in, 8 * 16)
            tr(bank[7][:, 0:48], vec_rows[0:48, :], ident[0:48, 0:48]).then_inc(vecT_ok, 1)

            def ready(what):
                n = number[what]
                if n >= R:
                    pe.wait_ge(evac, n - R + 1)
                return bank[n % R]

            def mod(v):
                if v == 1:
                    pe.wait_ge(cols_ok, 1)
                if v >= 2:
                    pe.wait_ge(mod_row, v - 1)
                for kk in range(KT // AK):
                    n = v * (KT // AK) + kk
                    pe.wait_ge(ada_in[n % ADA_RING], 16 * (n // ADA_RING + 1))
                    for k in range(AK):
                        for j in range(J):
                            last = mm(bank[6 + v % 2][H * j:H * j + H, 0:QW], c_rep[:, kk * AK + k, :],
                                      ada_ring[:, n % ADA_RING, k, QW * j:QW * j + QW],
                                      start=(kk == 0 and k == 0), stop=(kk == KT // AK - 1 and k == AK - 1))
                    last.then_inc(ada_used, 1)

            pe.wait_ge(xn_ok, TT)
            for k in range(R):
                ps = ready(("xT", k))
                for i in range(TT):
                    last = tr(ps[:, i * P:(i + 1) * P], xn[:, i, k * P:(k + 1) * P], ident[:, :])
                last.then_inc(prod, 1)
            pe.wait_ge(c_ok, 1)
            mod(0)
            mod(1)
            pe.wait_ge(mod_row, 2)
            for v in range(2):
                for m in range(QM):
                    at = (v * QM + m) * P
                    last = tr(bank[5][:, at:at + P], ada_rows[:, v, m * P:(m + 1) * P], ident[:, :])
            last.then_inc(mod_colT, 1)
            for k in range(R, KT):
                ps = ready(("xT", k))
                for i in range(TT):
                    last = tr(ps[:, i * P:(i + 1) * P], xn[:, i, k * P:(k + 1) * P], ident[:, :])
                last.then_inc(prod, 1)
            pe.wait_ge(evac, KT)

            def u_part(name, slot, count):
                pe.wait_ge(win_in[slot], 16 * count)
                for f in range(FT):
                    ps = ready((name, f))
                    for k in range(KT):
                        last = mm(ps[:, :], win_ring[:, slot, k, f * P:(f + 1) * P], hT[:, k, :], start=(k == 0),
                                  stop=(k == KT - 1))
                    last.then_inc(prod, 1)
                    yield f

            for _ in u_part("xa", 0, 1):
                pass
            for _ in u_part("xb", 1, 1):
                pass
            pe.wait_ge(bd_in, 4 * 16)
            ga_parts = u_part("ga", 0, 2)
            for f in range(FT):
                mod(2 + f)
                pe.wait_ge(conv_ok, f + 1)
                for n, name in enumerate(("r", "i")):
                    ps = ready((name, f))
                    mm(ps[:, :], gate_bd[:, n, f, :], conv_x[:, f, :], start=True, stop=True).then_inc(prod, 1)
                next(ga_parts)
            pe.wait_ge(pool_in, 16)
            for g in range(FT):
                pe.wait_ge(pool_ok, g + 1)
                ps = ready(("pool", g))
                mm(ps[:, :], pool_sb[:, g, :], catT[:, FT + g, :], start=True, stop=True).then_inc(prod, 1)
            pe.wait_ge(wout_in, 16)
            pe.wait_ge(gel_ok, FT)
            pe.wait_ge(evac, number["pool", FT - 1] + 1)
            pe.wait_ge(router_in, 32)
            for what in order[number["mix", 0, 0]:]:
                i = what[1]
                if what[0] == "hT":
                    pe.wait_ge(hn_ok, i + 1)
                if what[0] == "logits":
                    pe.wait_ge(evac, number["hT", i, 1] + 1)
                ps = ready(what)
                if what[0] == "mix":
                    n = what[2]
                    for k in range(KT):
                        last = mm(ps[:, :], catT[:, k, i * P:(i + 1) * P], W2[:, k, n * 512:(n + 1) * 512],
                                  start=(k == 0), stop=(k == KT - 1))
                elif what[0] == "hT":
                    for k in range(HALF):
                        col_at = (what[2] * HALF + k) * P
                        last = tr(ps[:, k * P:(k + 1) * P], hn[:, i % 2, col_at:col_at + P], ident[:, :])
                else:
                    for k in range(KT):
                        last = mm(ps[:, 0:E], h2T[:, i % 2, k, :], router_sb[:, k, :], start=(k == 0), stop=(k == KT - 1))
                last.then_inc(prod, 1)
                if what == ("mix", 0, 1):
                    pe.wait_ge(mod_row, 6)
                    for v in range(4):
                        if v:
                            pe.wait_ge(bc_ok, 2 * v)
                        for j in range(J):
                            last = mm(bank[4 + j // 2][:, (j % 2) * QW:(j % 2 + 1) * QW], ident[:, H * j:H * j + 1].to_broadcast([P, P]),
                                      ada_rows[:, 2 + v, :], start=True, stop=True)
                        last.then_inc(bc_ps, 1)

            pe.wait_ge(route_const, 6)
            pe.wait_ge(sel_ok, 1)
            pe.wait_ge(bc_ok, 8)
            for i in range(TT):
                for b in range(i + 1):
                    mm(bank[4][:, i * E:(i + 1) * E], upper if b == i else ones[:, :], sel[:, b, :], start=(b == 0),
                       stop=(b == i))
            for i in range(TT):
                last = mm(bank[5][:, 0:E], ones[:, :], sel[:, i, :], start=(i == 0), stop=(i == TT - 1))
            last.then_inc(rank_ok, 1)
            pe.wait_ge(slots_ok, 1)
            for n in range(TK):
                last = mm(bank[6][:, 0:2 * NQ], hot_t[:, n, :], slot_val[:, n, :, :].rearrange("p a b -> p (a b)"),
                          start=(n == 0), stop=(n == TK - 1))
            last.then_inc(table_ok, 1)

            def transpose_x(s, first=False):
                pe.wait_ge(xg_in, 32 * s + 32)
                if not first:
                    pe.wait_ge(xT_ok, s)
                for hf in range(2):
                    for m in range(QM):
                        at = (hf * QM + m) * P
                        last = tr(bank[2][:, at:at + P], xg[hf][:, m * P:(m + 1) * P], ident[:, :])
                last.then_inc(xT_ps, 1)

            def up(hf, slot, arrived):
                for k in range(KT):
                    pe.wait_ge(w1_in[slot][k], arrived)
                    for j in range(J):
                        last = mm(bank[hf][H * j:H * j + H, :], xT[:, hf, k % QM, H * (k // QM):H * (k // QM) + H],
                                  W1[:, slot, k, UW * j:UW * j + UW], start=(k == 0), stop=(k == KT - 1))
                last.then_inc(u_ps[hf], 1)

            def transpose_g(hf, n):
                pe.wait_ge(act_ok[hf], n + 1)
                for m in range(QM):
                    last = tr(gT_bank[hf][:, m * P:(m + 1) * P], act_g[:, hf, m * P:(m + 1) * P], ident[:, :])
                last.then_inc(gT_ps[hf], 1)

            def down(hf, n, arrived, c):
                if c == 0:
                    pe.wait_ge(gT_ok[hf], n + 1)
                pe.wait_ge(w2_in[c], arrived)
                for kk in (2 * c, 2 * c + 1):
                    for a in range(2):
                        k = a * HALF + kk
                        for piece in range(N2):
                            j = N2 * a + piece
                            last = mm(bank[4 + hf][H * j:H * j + H, :], gT[:, hf, k % QM, H * (k // QM):H * (k // QM) + H],
                                      W2[:, k, HW * piece:HW * piece + HW], start=(kk == 0), stop=(kk == HALF - 1))
                if c == 1:
                    last.then_inc(y_ps[hf], 1)

            for hf in range(2):
                pe.sem_inc(u_ps[hf], 1)
                pe.sem_inc(y_ps[hf], 1)
            transpose_x(0, first=True)
            pe.wait_ge(counts_ok, 3)
            step, full = pe.alloc_register("pe_step"), pe.alloc_register("pe_full")
            pe.reg_mov(step, 0)
            pe.reg_mov(full, 0)
            with pe.Fori(0, E // 2) as pair:
                for slot in range(2):
                    e = 2 * pair + slot
                    n_steps = pe.value_load(counts[0:1, 0, bass.ds(e, 1)], min_val=0, max_val=T // (2 * H))
                    n_halves = pe.value_load(counts[0:1, 1, bass.ds(e, 1)], min_val=0, max_val=T // H)
                    w1_arrived = pe.snap(16 * pair + 16, min_val=16, max_val=16 * E)
                    w2_arrived = pe.snap(32 * e + 32, min_val=32, max_val=32 * E)
                    with pe.If(n_steps > 0):
                        with pe.Fori(0, n_steps) as k:
                            s = pe.snap(step, min_val=0, max_val=STEPS_MAX)
                            n = pe.snap(full, min_val=0, max_val=STEPS_MAX)
                            pe.wait_ge(xT_ok, s + 1)
                            up(0, slot, w1_arrived)
                            with pe.If(2 * k + 1 < n_halves):
                                up(1, slot, w1_arrived)
                            transpose_g(0, s)
                            transpose_x(s + 1)
                            down(0, s, w2_arrived, 0)
                            with pe.If(2 * k + 1 < n_halves):
                                transpose_g(1, n)
                            down(0, s, w2_arrived, 1)
                            with pe.If(2 * k + 1 < n_halves):
                                down(1, n, w2_arrived, 0)
                                down(1, n, w2_arrived, 1)
                                pe.reg_add(full, full, 1)
                            pe.reg_add(step, step, 1)
                pe.nop()
    return nc


_INS = ["x", "c", "w_ada", "b_ada", "norm_mix_pre", "norm_mix_post", "w_in", "conv_w", "conv_b", "gate_a_w", "gate_a_b",
        "gate_x_w", "gate_x_b", "lru_lambda", "pool_w", "pool_b", "pool_scale", "w_out", "norm_ffn_pre",
        "norm_ffn_post", "router_w", "router_b", "expert_w1", "expert_b1", "expert_w2", "expert_b2"]


def kernel(**inputs):
    import numpy as _np
    import concourse.bacc as _bacc
    from concourse import mybir as _mybir
    from concourse.bass_utils import run_bass_kernel_spmd as _run

    nc = _bacc.Bacc("TRN2", target_bir_lowering=False, num_devices=1)
    arrays, args = {}, []
    for name in _INS:
        a = _np.ascontiguousarray(inputs[name])
        arrays[f"in_{name}"] = a
        args.append(nc.dram_tensor(f"in_{name}", a.shape, _mybir.dt.from_np(a.dtype), kind="ExternalInput").ap())
    out = nc.dram_tensor("out_0", arrays["in_x"].shape, _mybir.dt.float32, kind="ExternalOutput").ap()
    hybrid_layer(nc, *args, out)
    r = _run(nc, [arrays], core_ids=[0])
    return r.results[0]["out_0"]
```

```python
import concourse.bass as bass
from concourse import mybir
from contextlib import ExitStack


def hybrid_layer(nc, x, c, w_ada, b_ada, norm_mix_pre, norm_mix_post, w_in, conv_w, conv_b, gate_a_w, gate_a_b,
                 gate_x_w, gate_x_b, lru_lambda, pool_w, pool_b, pool_scale, w_out, norm_ffn_pre, norm_ffn_post,
                 router_w, router_b, expert_w1, expert_b1, expert_w2, expert_b2, out):
    fp32, i32, u32 = mybir.dt.float32, mybir.dt.int32, mybir.dt.uint32
    ALU, ACT, AX = mybir.AluOpType, mybir.ActivationFunctionType, mybir.AxisListType

    P = 128
    T, D = x.shape[1], x.shape[2]
    TT = T // P
    KT = D // P
    E, F2 = expert_w1.shape[1], expert_w1.shape[3]
    F = F2 // 2
    TOPK = 4
    FT = w_in.shape[2] // P // 3
    CONV = conv_w.shape[1]
    LRU_C, EPS, LIMIT, ALPHA = 8.0, 1e-6, 7.0, 1.702
    J = 4
    H = 32
    QW = D // J
    QM = QW // P
    UW = F2 // J
    N2 = 2
    HW = D // N2
    YP = N2 * H
    STEPS_MAX = T * TOPK // (2 * H) + E
    NQ = 2 * STEPS_MAX + 4
    EMPTY = 1 << 20
    PADC, PADP = CONV - 1, 15

    h_rows = nc.dram_tensor("h_rows", (T * J, QW), fp32).ap()
    y_rows = nc.dram_tensor("y_rows", (T * TOPK * N2, HW), fp32).ap()
    h_store = h_rows.rearrange("(t j) c -> t (j c)", j=J)
    y_load = y_rows.rearrange("(t r) c -> t (r c)", r=TOPK * N2)

    w_ada_v = w_ada[0].rearrange("(k p) n -> p k n", p=P)
    w_in_v = w_in[0].rearrange("(k p) n -> p k n", p=P)
    w_out_v = w_out[0].rearrange("(k p) n -> p k n", p=P)
    w1_v = expert_w1[0].rearrange("e (k p) n -> e p k n", p=P)
    w2_v = expert_w2[0].rearrange("e (k p) n -> e p k n", p=P)

    ctx = ExitStack()
    with ctx:
        def sb(name, shape, dt=fp32):
            return ctx.enter_context(nc.sbuf_tensor(name, shape, dt))

        def sem(name):
            return ctx.enter_context(nc.semaphore(name))

        def sems(name, n):
            return [sem(f"{name}{i}") for i in range(n)]

        W1 = sb("W1", [P, 2, KT, F2])
        W2 = sb("W2", [P, KT, D])
        OV = sb("OV", [P, 6656])
        x1 = sb("x1", [P, TT, D])
        gate_f_bc = sb("gate_f_bc", [P, D])
        ident = sb("ident", [P, P])
        ones = sb("ones", [P, P])
        gates = sb("gates", [P, TT, TOPK])
        src_cur = sb("src_cur", [P, 2], i32)
        dst_cur = [sb("dst_cur_a", [YP, 1], i32), sb("dst_cur_b", [YP, 1], i32)]
        stat = sb("stat", [P, 8, TT])
        router_bias = sb("router_bias", [P, E])

        def carver(area):
            at = [0]

            def take(*shape):
                n = 1
                for size in shape:
                    n *= size
                v = area[:, at[0]:at[0] + n]
                at[0] += n
                assert at[0] <= area.shape[1], (at[0], area.shape)
                if len(shape) > 1:
                    names = "abcd"[:len(shape)]
                    v = v.rearrange(f"p ({' '.join(names)}) -> p {' '.join(names)}", **dict(zip(names, shape)))
                return v
            return take

        def flat(v):
            return v.rearrange("p a b -> p (a b)")

        HALF = KT // 2
        A_lo, A_hi = flat(W1[:, 0, 0:HALF, :]), flat(W1[:, 0, HALF:KT, :])
        B_lo, B_hi = flat(W1[:, 1, 0:HALF, :]), flat(W1[:, 1, HALF:KT, :])

        ADA_RING, AK = 3, 2
        take = carver(A_lo)
        ada_ring = take(ADA_RING, AK, D)
        gate_bd = take(2, FT, P)
        pool_sb = take(FT, P)
        inv_count = take(PADP + 1)
        mod_col = take(2, J, QM)
        lru_c = take(8, FT)
        pool_pb = take(FT)
        c_sig = take(KT)
        take = carver(A_hi)
        conv_x = take(FT, T)
        rgate = take(T)
        igate = take(2, T)
        decay = take(2, T)
        decay2 = take(2, T)
        tanh_m = take(2, T)
        xa_pad = take(2, T + PADC)
        c_rep = take(KT, H)
        cols = take(48)
        win_ring = carver(B_lo)(2, KT, FT * P)
        take = carver(B_lo)
        mixb = take(2, D)
        junk = take(D)
        hn = take(2, D)
        h2T = take(2, KT, P)
        take = carver(B_hi)
        hT = take(KT, T)
        xb_pad = take(2, T + PADP)
        sums = take(2, T + PADP)
        ga = take(2, T)
        gel = take(T)
        B_HI = B_hi.shape[1]
        router_sb = carver(B_hi[:, B_HI - KT * E:])(KT, E)
        vec_rows = carver(B_hi[:, B_HI - KT * E - P:])(P)
        bc = carver(B_hi[:, KT * T:])(3, D)
        TK = TT * TOPK
        take = carver(B_hi)
        slot_val = take(TK, NQ)
        hot_t = take(TK, P)
        hot_e = take(TT, TOPK, E)
        route_tmp = take(TK, E)
        catT = carver(OV)(KT, T)
        xn = carver(OV)(TT, D)
        take = carver(OV[:, KT * T:])
        ada_rows = take(6, QW)
        gain_rows = take(4, QW)
        take = carver(OV[:, KT * T:])
        iota_q = take(NQ)
        iota_t = take(P)
        iota_e = take(E)
        upper = take(P)
        tok_no = take(TK)
        j_off = take(2)
        logits = take(TT, E)
        top = take(TT, 8)
        top_i = take(TT, 8).bitcast(u32)
        sel = take(TT, E)
        slot_e = take(TT, E)
        exp_f = take(4, E)
        exp_i = take(3, E).bitcast(i32)
        tk_f = take(4, TK)
        tk_i = take(3, TK).bitcast(i32)
        top_d = take(TT, TOPK)
        top_e = take(TT, TOPK)
        idx_f = take(2, NQ)
        idx_e = take(NQ)
        idx_n = take(NQ).bitcast(i32)
        take = carver(OV)
        xg = [take(QW), take(QW)]
        xT = take(2, QM, P)
        b1_bc = take(2, UW)
        b2_and_y1 = take(2, HW)
        b2_bc = b2_and_y1[YP:2 * YP]
        y_part = b2_and_y1[0:YP]
        u_sb = take(2, UW)
        act_g = take(2, QW)
        gT = take(2, QM, P)
        y_sb = [take(HW)[0:YP], take(HW)[0:YP]]
        idx = take(2, NQ // 2, 2).bitcast(i32)
        counts = OV[0:1, 6656 - 4 * E:6656].rearrange("p (a e) -> p a e", a=4).bitcast(i32)
        y_all = carver(flat(W1[:, 0, :, :]))(TT, TOPK, D)
        fin = carver(B_lo)(TT, D)
        fin_junk = carver(B_hi)(D)

        bank = [ctx.enter_context(nc.psum_tensor(f"bank{i}", [P, 512], fp32)) for i in range(8)]
        R = 4

        order = [("xT", k) for k in range(KT)] + [("xa", f) for f in range(FT)] + [("xb", f) for f in range(FT)]
        for f in range(FT):
            order += [("r", f), ("i", f), ("ga", f)]
        order += [("pool", f) for f in range(FT)]
        for i in range(TT):
            order.append(("mix", i, 0))
            if i >= 2:
                order.append(("logits", i - 2))
            order.append(("mix", i, 1))
            if i >= 1:
                order += [("hT", i - 1, 0), ("hT", i - 1, 1)]
        order += [("logits", TT - 2), ("hT", TT - 1, 0), ("hT", TT - 1, 1), ("logits", TT - 1)]
        number = {what: n for n, what in enumerate(order)}

        x_in = sems("x_in", TT)
        vec_in = sem("vec_in")
        ada_in = sems("ada_in", ADA_RING)
        win_in = sems("win_in", 2)
        wout_in = sem("wout_in")
        rows_in = sem("rows_in")
        bd_in = sem("bd_in")
        pool_in = sem("pool_in")
        router_in = sem("router_in")
        window_ok = sem("window_ok")
        pool_const = sem("pool_const")
        ident_ok = sem("ident_ok")
        pads_ok = sem("pads_ok")
        x_sq = sem("x_sq")
        xn_ok = sem("xn_ok")
        vecT_ok = sem("vecT_ok")
        cols_ok = sem("cols_ok")
        c_sig_ok = sem("c_sig_ok")
        c_ok = sem("c_ok")
        lam_abs_ok = sem("lam_abs_ok")
        lam_exp_ok = sem("lam_exp_ok")
        lru_c_ok = sem("lru_c_ok")
        ada_used = sem("ada_used")
        mod_row = sem("mod_row")
        mod_colT = sem("mod_colT")
        mod_col_ok = sem("mod_col_ok")
        prod = sem("prod")
        evac = sem("evac")
        conv_ok = sem("conv_ok")
        pool_ok = sem("pool_ok")
        lru_in = sem("lru_in")
        lru_ok = sem("lru_ok")
        gel_in = sem("gel_in")
        gel_sig = sem("gel_sig")
        gel_ok = sem("gel_ok")
        bc_ps = sem("bc_ps")
        bc_ok = sem("bc_ok")
        x1_ok = sem("x1_ok")
        x1_sq = sem("x1_sq")
        hn_ok = sem("hn_ok")
        h_stored = sems("h_stored", 2)
        route_const = sem("route_const")
        sel_ok = sem("sel_ok")
        rank_ok = sem("rank_ok")
        top_ok = sem("top_ok")
        top_exp = sem("top_exp")
        counts_ok = sem("counts_ok")
        slots_ok = sem("slots_ok")
        table_ok = sem("table_ok")
        idx_ok = sem("idx_ok")
        ms_ok = sem("ms_ok")
        rms_ok = sem("rms_ok")
        m2_ok = sem("m2_ok")
        root_ok = sem("root_ok")
        apart_n = sem("apart_n")
        dve_chain = sem("dve_chain")
        act_chain = sem("act_chain")
        pool_chain = sem("pool_chain")
        w1_in = [sems(f"w1_in{s}_", KT) for s in range(2)]
        w2_in = sems("w2_in", 2)
        bias_in = sems("bias_in", 2)
        xg_in = sem("xg_in")
        xT_ps = sem("xT_ps")
        xT_ok = sem("xT_ok")
        w1_used = sem("w1_used")
        w2_used = sem("w2_used")
        u_ps = sems("u_ps", 2)
        u_ok = sems("u_ok", 2)
        lin_ok = sems("lin_ok", 2)
        glu_ok = sems("glu_ok", 2)
        sig_ok = sems("sig_ok", 2)
        mul_ok = sems("mul_ok", 2)
        act_ok = sems("act_ok", 2)
        gT_ps = sems("gT_ps", 2)
        gT_ok = sems("gT_ok", 2)
        y_ps = sems("y_ps", 2)
        y_part_ok = sems("y_part_ok", 2)
        y_ok = sems("y_ok", 2)
        y_stored = sems("y_stored", 2)
        src_ok = sem("src_ok")
        dst_ok = sems("dst_ok", 2)
        moe_done = sem("moe_done")
        y_in = sems("y_in", TT)
        y_first = sem("y_first")
        f_sum = sem("f_sum")
        f_sq = sem("f_sq")
        f_scaled = sem("f_scaled")
        out_ok = sem("out_ok")
        out_stored = sem("out_stored")

        f_chain = sem("f_chain")
        COL = {name: CONV * FT + n * FT for n, name in enumerate(
            ("conv_b", "gate_a_b", "gate_x_b", "lru_lambda", "pool_b", "pool_scale", "c"))}
        c_col = cols[:, COL["c"]:COL["c"] + KT]
        gT_bank = [bank[3], bank[6]]
        GELU = 2.0 * (2.0 / 3.141592653589793) ** 0.5

        def u_parts(hf):
            return u_sb[:, hf, :].rearrange("p (n two) -> p n two", two=2)

        def col(name, f):
            return cols[:, COL[name] + f:COL[name] + f + 1]

        def flat3(v):
            return v.rearrange("p a b c -> p (a b c)")

        block = ctx.enter_context(nc.Block())

        def apart(engine):
            engine.sem_inc(apart_n, 1)

        def linker(engine, chain):
            n = [0]

            def link(instruction):
                n[0] += 1
                instruction.then_inc(chain, 1)
                engine.wait_ge(chain, n[0])
            return link

        def load_w1(sp, e, slot, k):
            sp.dma_start(W1[:, slot, k, :], w1_v[bass.ds(e, 1), :, k, :].rearrange("e p n -> p (e n)"))\
                .then_inc(w1_in[slot][k], 16)

        W2_halves = W2[:, :, :].rearrange("p (a k) n -> p a k n", a=2)

        def load_w2(engine, e, c, experts=w2_v):
            for a in range(2):
                k = a * HALF + 2 * c
                src = experts[bass.ds(e, 1), :, k:k + 2, :].rearrange("e p k n -> p (e k) n")
                engine.dma_start(W2_halves[:, a, 2 * c:2 * c + 2, :], src).then_inc(w2_in[c], 16)

        def load_bias(sp, e, slot):
            for j in range(J):
                sp.dma_start(b1_bc[H * j:H * j + H, slot, :], expert_b1[0, bass.ds(e, 1), UW * j:UW * j + UW]
                             .to_broadcast([H, UW])).then_inc(bias_in[slot], 16)
            for n in range(N2):
                sp.dma_start(b2_bc[H * n:H * n + H, slot, :], expert_b2[0, bass.ds(e, 1), HW * n:HW * n + HW]
                             .to_broadcast([H, HW])).then_inc(bias_in[slot], 16)
        BIAS_INC = (J + N2) * 16

        @block.sync
        def _(sp):
            for i in range(TT):
                sp.dma_start(x1[:, i, :], x[0, i * P:(i + 1) * P, :]).then_inc(x_in[i], 16)

            def load_ada(n):
                v, kk = n // (KT // AK), n % (KT // AK)
                if n >= ADA_RING:
                    sp.wait_ge(ada_used, n - ADA_RING + 1)
                sp.dma_start(ada_ring[:, n % ADA_RING, :, :],
                             w_ada_v[:, kk * AK:(kk + 1) * AK, v * D:(v + 1) * D]).then_inc(ada_in[n % ADA_RING], 16)

            def load_win(part, slot):
                sp.dma_start(win_ring[:, slot, :, :], w_in_v[:, :, part * FT * P:(part + 1) * FT * P])\
                    .then_inc(win_in[slot], 16)

            PIECES = KT // AK
            sp.wait_ge(vec_in, 8 * 16)
            for n in range(2 * PIECES):
                load_ada(n)
            load_win(0, 0)
            load_win(2, 1)
            for n in range(2 * PIECES, 3 * PIECES):
                load_ada(n)
            sp.wait_ge(prod, number["xa", FT - 1] + 1)
            load_win(1, 0)
            sp.dma_start(W2[:, :, :], w_out_v).then_inc(wout_in, 16)
            for n in range(3 * PIECES, 6 * PIECES):
                load_ada(n)
            sp.wait_ge(evac, number["pool", FT - 1] + 1)
            sp.wait_ge(ada_used, 6 * PIECES)
            sp.wait_ge(lru_ok, FT)
            for k in range(KT):
                load_w1(sp, 0, 0, k)
            sp.wait_ge(prod, number["mix", TT - 1, 1] + 1)
            for c in range(2):
                load_w2(sp, 0, c)
            for s in range(2):
                sp.wait_ge(h_stored[s], 16 * TT // 2)
            sp.wait_ge(evac, number["logits", TT - 1] + 1)
            sp.wait_ge(counts_ok, 4)
            for k in range(KT):
                sp.sem_inc(w1_in[1][k], 16)
            sp.sem_inc(bias_in[1], BIAS_INC)
            load = sp.value_load(counts[0:1, 3, 1:2], min_val=0, max_val=16)
            with sp.If(load > 0):
                for k in range(HALF):
                    load_w1(sp, 1, 1, k)
            sp.wait_ge(idx_ok, 1)
            load_bias(sp, 0, 0)
            with sp.If(load > 0):
                for k in range(HALF, KT):
                    load_w1(sp, 1, 1, k)
                load_bias(sp, 1, 1)
            step, landed = sp.alloc_register("sp_step"), [sp.alloc_register(f"sp_landed{v}") for v in range(2)]
            sp.reg_mov(step, 0)
            full = sp.alloc_register("sp_full")
            sp.reg_mov(full, 0)
            sp.reg_mov(landed[0], 16)
            sp.reg_mov(landed[1], 16)
            sp.reg_add(landed[1], landed[1], load)
            with sp.Fori(1, E // 2) as pair:
                for slot in range(2):
                    e = 2 * pair + slot
                    n_steps = sp.value_load(counts[0:1, 0, bass.ds(e - 2, 1)], min_val=0, max_val=T // (2 * H))
                    sp.reg_add(step, step, n_steps)
                    n_full = sp.value_load(counts[0:1, 2, bass.ds(e - 2, 1)], min_val=0, max_val=T // (2 * H))
                    sp.reg_add(full, full, n_full)
                    load = sp.value_load(counts[0:1, 3, bass.ds(e, 1)], min_val=0, max_val=16)
                    with sp.If(load > 0):
                        s = sp.snap(step, min_val=0, max_val=STEPS_MAX)
                        n = sp.snap(full, min_val=0, max_val=STEPS_MAX)
                        for k in range(KT):
                            if k < 2:
                                for v in range(2):
                                    value = sp.snap(landed[v], min_val=16, max_val=16 * E)
                                    sp.wait_ge(w1_in[v][KT - 2 + k], value)
                                    apart(sp)
                            else:
                                value = sp.snap(landed[slot], min_val=16, max_val=16 * E)
                                sp.wait_ge(w1_in[slot][k - 2], value)
                                apart(sp)
                            if k == 1:
                                sp.reg_add(landed[slot], landed[slot], 16)
                            sp.wait_ge(w1_used, KT * s + (k + 1))
                            apart(sp)
                            load_w1(sp, e, slot, k)
                        sp.wait_ge(y_ok[0], s + 1)
                        apart(sp)
                        sp.wait_ge(y_ok[1], n + 1)
                        apart(sp)
                        value = sp.snap(landed[slot], min_val=16, max_val=16 * E)
                        sp.wait_ge(bias_in[slot], (J + N2) * value - BIAS_INC)
                        apart(sp)
                        load_bias(sp, e, slot)
                    sp.nop()
            sp.wait_ge(moe_done, 1)
            for i in range(TT):
                sp.dma_start(y_all[:, i, :, :].rearrange("p k d -> p (k d)"), y_load[i * P:(i + 1) * P, :])\
                    .then_inc(y_in[i], 16)
            for i in range(TT):
                sp.wait_ge(out_ok, i + 1)
                sp.dma_start(out[0, i * P:(i + 1) * P, :], fin[:, i, :]).then_inc(out_stored, 16)
            sp.wait_ge(out_stored, 16 * TT)

        @block.gpsimd
        def _(pool):
            link = linker(pool, pool_chain)
            link(nc.gpsimd.memset(ident[:, :], 0.0))
            nc.gpsimd.affine_select(out=ident[:, :], in_=ident[:, :], compare_op=ALU.not_equal, fill=1.0, base=0,
                                    pattern=[[-1, P]], channel_multiplier=1).then_inc(ident_ok, 1)
            nc.gpsimd.memset(ones[:, :], 1.0).then_inc(ident_ok, 1)
            for j in range(J):
                part = slice(H * j, H * j + H)
                src = b_ada[0:1, :].rearrange("a (v q c) -> a q v c", v=6, q=J)[:, j, :, :]
                pool.dma_start(ada_rows[part, :, :], src.to_broadcast([H, 6, QW])).then_inc(rows_in, 16)
                for g, gain in enumerate((norm_mix_pre, norm_mix_post, norm_ffn_pre, norm_ffn_post)):
                    pool.dma_start(gain_rows[part, g, :], gain[0:1, QW * j:QW * j + QW].to_broadcast([H, QW]))\
                        .then_inc(rows_in, 16)
            link(nc.gpsimd.memset(gate_bd[:, :, :, :], 0.0))
            for n, w in enumerate((gate_a_w, gate_x_w)):
                for par in range(2):
                    lo = par * (P // 2)
                    pool.dma_start(gate_bd[lo:lo + P // 2, n, :, lo:lo + P // 2],
                                   w[0].rearrange("(f r) i o -> r i f o", r=2)[par]).then_inc(bd_in, 16)
            pool.dma_start(pool_sb, pool_w[0].rearrange("g c d -> c g d")).then_inc(pool_in, 16)
            pool.dma_start(router_sb, router_w[0].rearrange("(k p) e -> p k e", p=P)).then_inc(router_in, 16)
            pool.dma_start(router_bias[:, :], router_b[0:1, :].to_broadcast([P, E])).then_inc(router_in, 16)
            nc.gpsimd.memset(xb_pad[:, :, 0:PADP], 0.0).then_inc(pads_ok, 1)
            nc.gpsimd.iota(inv_count, [[1, PADP + 1]], base=1, channel_multiplier=0,
                           allow_small_or_imprecise_dtypes=True).then_inc(window_ok, 1)
            pool.wait_ge(pool_const, 1)
            L = T + PADP
            for g in range(FT):
                w = 2 ** (g + 1)
                pool.wait_ge(evac, number["xb", g] + 1)
                cur = xb_pad[:, g % 2, :]
                for level in range(g + 1):
                    s, lo = 2 ** level, 2 ** (level + 1) - 1
                    nxt = sums[:, level % 2, :]
                    link(nc.gpsimd.tensor_tensor(nxt[:, lo:L], cur[:, lo:L], cur[:, lo - s:L - s], ALU.add))
                    cur = nxt
                p_out, xb = catT[:, FT + g, :], xb_pad[:, g % 2, PADP:L]
                link(nc.gpsimd.tensor_scalar(p_out, cur[:, PADP:L], 1.0 / w, None, ALU.mult))
                link(nc.gpsimd.tensor_tensor(p_out[:, 0:w - 1], cur[:, PADP:PADP + w - 1], inv_count[:, 0:w - 1], ALU.mult))
                nc.gpsimd.tensor_tensor(p_out, p_out, xb, ALU.subtract).then_inc(pool_ok, 1)
                pool.wait_ge(pool_ok, g + 1)
            pool.wait_ge(bc_ps, 4)
            IMP = dict(allow_small_or_imprecise_dtypes=True)
            nc.gpsimd.iota(iota_q, [[1, NQ]], base=0, channel_multiplier=0, **IMP).then_inc(route_const, 1)
            nc.gpsimd.iota(iota_t, [[0, J], [1, H]], base=0, channel_multiplier=0, **IMP).then_inc(route_const, 1)
            nc.gpsimd.iota(iota_e, [[1, E]], base=0, channel_multiplier=0, **IMP).then_inc(route_const, 1)
            nc.gpsimd.iota(tok_no, [[P * TOPK, TT], [1, TOPK]], base=1, channel_multiplier=TOPK, **IMP)\
                .then_inc(route_const, 1)
            link(nc.gpsimd.memset(upper, 1.0))
            nc.gpsimd.affine_select(out=upper, in_=upper, compare_op=ALU.is_gt, fill=0.0, base=0,
                                    pattern=[[1, P]], channel_multiplier=-1).then_inc(route_const, 1)
            for i in range(TT):
                pool.wait_ge(hn_ok, i + 1)
                pool.dma_start(h_store[i * P:(i + 1) * P, :], hn[:, i % 2, :]).then_inc(h_stored[i % 2], 16)
            for s in range(2):
                pool.wait_ge(h_stored[s], 16 * TT // 2)
            pool.wait_ge(idx_ok, 1)
            link(nc.gpsimd.memset(xg[0], 0.0))
            link(nc.gpsimd.memset(xg[1], 0.0))

            def gather(step):
                nc.gpsimd.tensor_copy(src_cur[:, :].rearrange("p (a b) -> p a b", a=1), idx[:, 0, bass.ds(step, 1), :])\
                    .then_inc(src_ok, 1)
                pool.wait_ge(src_ok, step + 1)
                apart(pool)
                for hf in range(2):
                    pool.indirect_dma_start(xg[hf], None, h_rows, bass.IndirectOffsetOnAxis(ap=src_cur[:, hf:hf + 1], axis=0),
                                            bounds_check=T * J - 1, oob_is_err=False).then_inc(xg_in, 16)

            def scatter(hf, n, step):
                pool.wait_ge(y_ok[hf], n + 1)
                nc.gpsimd.tensor_copy(dst_cur[hf][:, :].rearrange("p (a b) -> p a b", a=1),
                                      idx[0:YP, 1, bass.ds(step, 1), hf:hf + 1]).then_inc(dst_ok[hf], 1)
                pool.wait_ge(dst_ok[hf], n + 1)
                apart(pool)
                pool.indirect_dma_start(y_rows, bass.IndirectOffsetOnAxis(ap=dst_cur[hf][:, 0:1], axis=0), y_sb[hf], None,
                                        bounds_check=T * TOPK * N2 - 1, oob_is_err=False).then_inc(y_stored[hf], 16)

            NOTHING = NQ // 2 - 1
            for hf in range(2):
                nc.gpsimd.memset(y_sb[hf], 0.0).then_inc(y_ok[hf], 1)
            scatter(1, 0, NOTHING)
            gather(0)
            step, full = pool.alloc_register("pool_step"), pool.alloc_register("pool_full")
            before, before_halves = pool.alloc_register("pool_before"), pool.alloc_register("pool_before_halves")
            pool.reg_mov(step, 0)
            pool.reg_mov(full, 0)
            pool.reg_mov(before, NOTHING)
            pool.reg_mov(before_halves, 0)

            def scatter_before():
                s = pool.snap(step, min_val=0, max_val=STEPS_MAX)
                at = pool.snap(before, min_val=0, max_val=NOTHING)
                scatter(0, s, at)
                with pool.If(pool.snap(before_halves, min_val=0, max_val=T // H) > 1):
                    n = pool.snap(full, min_val=0, max_val=STEPS_MAX)
                    at = pool.snap(before, min_val=0, max_val=NOTHING)
                    scatter(1, n + 1, at)
                    pool.reg_add(full, full, 1)

            with pool.Fori(0, E) as e:
                n_steps = pool.value_load(counts[0:1, 0, bass.ds(e, 1)], min_val=0, max_val=T // (2 * H))
                n_halves = pool.value_load(counts[0:1, 1, bass.ds(e, 1)], min_val=0, max_val=T // H)
                with pool.If(n_steps > 0):
                    with pool.Fori(0, n_steps) as k:
                        s = pool.snap(step, min_val=0, max_val=STEPS_MAX)
                        pool.wait_ge(xT_ps, s + 1)
                        apart(pool)
                        gather(s + 1)
                        scatter_before()
                        pool.reg_mov(before, step)
                        pool.reg_mov(before_halves, n_halves - 2 * k)
                        pool.reg_add(step, step, 1)
                pool.nop()
            scatter_before()
            s = pool.snap(step, min_val=0, max_val=STEPS_MAX)
            n = pool.snap(full, min_val=0, max_val=STEPS_MAX)
            pool.wait_ge(y_stored[0], 16 * s + 16)
            pool.wait_ge(y_stored[1], 16 * n + 16)
            apart(pool)
            pool.drain().then_inc(moe_done, 1)

            for i in range(TT):
                pool.wait_ge(f_scaled, i + 1)
                nc.gpsimd.tensor_tensor(fin[:, i, :], fin[:, i, :], x1[:, i, :], ALU.add).then_inc(out_ok, 1)

        @block.scalar
        def _(act):
            link = linker(act, act_chain)
            vecs = [(0, conv_w[0].rearrange("k (f p) -> (k f) p", p=P))]
            at = CONV * FT
            for v in (conv_b, gate_a_b, gate_x_b, lru_lambda, pool_b, pool_scale):
                vecs.append((at, v[0].rearrange("(f p) -> f p", p=P)))
                at += FT
            vecs.append((at, c[0].rearrange("(k p) -> k p", p=P)))
            for at, v in vecs:
                act.dma_start(vec_rows[at:at + v.shape[0], :], v).then_inc(vec_in, 16)
            for i in range(TT):
                act.wait_ge(x_in[i], 16)
                nc.scalar.activation(hT[:, 2 * i:2 * i + 2, :].rearrange("p a b -> p (a b)"), x1[:, i, :], ACT.Square,
                                     accum_out=stat[:, 0, i:i + 1]).then_inc(x_sq, 1)
            roots = [0]

            def root(v):
                roots[0] += 1
                act.wait_ge(ms_ok, roots[0])
                nc.scalar.activation(v, v, ACT.Sqrt).then_inc(rms_ok, 1)

            act.wait_ge(cols_ok, 1)
            nc.scalar.activation(c_sig, c_col, ACT.Sigmoid).then_inc(c_sig_ok, 1)
            for i in range(TT):
                root(stat[:, 1, i:i + 1])
            act.wait_ge(lam_abs_ok, 1)
            nc.scalar.activation(lru_c[:, 1, :], lru_c[:, 0, :], ACT.Exp, scale=-1.0).then_inc(lam_exp_ok, 1)

            def take_out(what):
                n = number[what]
                act.wait_ge(prod, n + 1)
                return bank[n % R]

            act.wait_ge(mod_col_ok, 1)
            act.wait_ge(x_sq, TT)
            for k in range(KT):
                ps = take_out(("xT", k))
                nc.scalar.activation(hT[:, k, :], ps[:, :], ACT.Identity, bias=mod_col[:, 0, k // QM, k % QM:k % QM + 1],
                                     scale=mod_col[:, 1, k // QM, k % QM:k % QM + 1]).then_inc(evac, 1)
            for f in range(FT):
                ps = take_out(("xa", f))
                if f >= 2:
                    act.wait_ge(conv_ok, f - 1)
                nc.scalar.activation(xa_pad[:, f % 2, PADC:], ps[:, :], ACT.Copy).then_inc(evac, 1)
            act.wait_ge(pads_ok, 1)
            for f in range(FT):
                ps = take_out(("xb", f))
                if f >= 2:
                    act.wait_ge(pool_ok, f - 1)
                nc.scalar.activation(xb_pad[:, f % 2, PADP:], ps[:, :], ACT.Copy).then_inc(evac, 1)
            act.wait_ge(lru_c_ok, 1)
            for f in range(FT):
                ps = take_out(("r", f))
                if f:
                    act.wait_ge(lru_in, 3 * f)
                nc.scalar.activation(rgate, ps[:, :], ACT.Sigmoid, bias=col("gate_a_b", f)).then_inc(evac, 1)
                ps = take_out(("i", f))
                if f >= 2:
                    act.wait_ge(lru_ok, f - 1)
                nc.scalar.activation(igate[:, f % 2, :], ps[:, :], ACT.Sigmoid, bias=col("gate_x_b", f)).then_inc(evac, 1)
                act.wait_ge(evac, number["i", f] + 1)
                nc.scalar.activation(decay[:, f % 2, :], rgate, ACT.Exp, scale=lru_c[:, 5, f:f + 1]).then_inc(lru_in, 1)
                nc.scalar.activation(decay2[:, f % 2, :], rgate, ACT.Exp, scale=lru_c[:, 6, f:f + 1]).then_inc(lru_in, 1)
                nc.scalar.activation(tanh_m[:, f % 2, :], rgate, ACT.Tanh, scale=lru_c[:, 7, f:f + 1]).then_inc(lru_in, 1)
                act.wait_ge(m2_ok, f + 1)
                nc.scalar.activation(tanh_m[:, f % 2, :], tanh_m[:, f % 2, :], ACT.Sqrt).then_inc(root_ok, 1)
                ps = take_out(("ga", f))
                if f >= 2:
                    act.wait_ge(gel_ok, f - 1)
                nc.scalar.activation(ga[:, f % 2, :], ps[:, :], ACT.Copy).then_inc(evac, 1)
                if f >= 1:
                    act.wait_ge(gel_in, f)
                    nc.scalar.activation(gel, gel, ACT.Sigmoid, scale=GELU).then_inc(gel_sig, 1)
            act.wait_ge(gel_in, FT)
            nc.scalar.activation(gel, gel, ACT.Sigmoid, scale=GELU).then_inc(gel_sig, 1)
            for f in range(FT):
                ps = take_out(("pool", f))
                nc.scalar.activation(catT[:, FT + f, :], ps[:, :], ACT.Identity, bias=pool_pb[:, f:f + 1],
                                     scale=col("pool_scale", f)).then_inc(evac, 1)

            bc_to = [bc[:, 0, :], bc[:, 1, :], bc[:, 2, :], gate_f_bc[:, :]]
            act.wait_ge(gel_ok, FT)
            act.wait_ge(pool_ok, FT)
            for v in range(4):
                act.wait_ge(bc_ps, v + 1)
                for n in range(2):
                    nc.scalar.activation(bc_to[v][:, n * 512:(n + 1) * 512], bank[4 + 2 * (v % 2) + n][:, :], ACT.Copy)\
                        .then_inc(bc_ok, 1)

            def x1_square(i):
                act.wait_ge(x1_ok, i + 1)
                nc.scalar.activation(junk, x1[:, i, :], ACT.Square, accum_out=stat[:, 5, i:i + 1]).then_inc(x1_sq, 1)
                act.wait_ge(x1_sq, i + 1)
                root(stat[:, 6, i:i + 1])

            for what in order[number["mix", 0, 0]:]:
                ps = take_out(what)
                i = what[1]
                if what[0] == "mix":
                    n = what[2]
                    if i >= 2:
                        act.wait_ge(x1_ok, i - 1)
                    link(nc.scalar.activation(junk[:, 0:512], ps[:, :], ACT.Square, accum_out=stat[:, 2 + n, i:i + 1]))
                    nc.scalar.activation(mixb[:, i % 2, n * 512:(n + 1) * 512], ps[:, :], ACT.Copy).then_inc(evac, 1)
                    if n == 1:
                        root(stat[:, 4, i:i + 1])
                        if i == 0:
                            x1_square(i)
                elif what[0] == "hT":
                    n = what[2]
                    nc.scalar.activation(h2T[:, i % 2, n * HALF:(n + 1) * HALF, :].rearrange("p a b -> p (a b)"), ps[:, :],
                                         ACT.Copy).then_inc(evac, 1)
                    if n == 1 and i + 1 < TT:
                        x1_square(i + 1)
                else:
                    nc.scalar.activation(logits[:, i, :], ps[:, 0:E], ACT.Copy).then_inc(evac, 1)
            act.wait_ge(top_ok, 1)
            nc.scalar.activation(top_e, top_d, ACT.Exp).then_inc(top_exp, 1)

            act.preload_act_table(ACT.Sigmoid)

            def take_xT(s):
                act.wait_ge(xT_ps, s + 1)
                nc.scalar.activation(flat3(xT), bank[2][:, :], ACT.Copy).then_inc(xT_ok, 1)

            def sigmoid(hf, n):
                act.wait_ge(glu_ok[hf], n + 1)
                nc.scalar.activation(act_g[:, hf, :], u_parts(hf)[:, :, 0], ACT.Sigmoid, scale=ALPHA).then_inc(sig_ok[hf], 1)

            def take_gT(hf, n):
                act.wait_ge(gT_ps[hf], n + 1)
                nc.scalar.activation(flat(gT[:, hf, :, :]), gT_bank[hf][:, 0:QW], ACT.Copy).then_inc(gT_ok[hf], 1)

            take_xT(0)
            act.wait_ge(counts_ok, 4)
            step, full = act.alloc_register("act_step"), act.alloc_register("act_full")
            act.reg_mov(step, 0)
            act.reg_mov(full, 0)

            def expert(e):
                n_steps = act.value_load(counts[0:1, 0, bass.ds(e, 1)], min_val=0, max_val=T // (2 * H))
                n_halves = act.value_load(counts[0:1, 1, bass.ds(e, 1)], min_val=0, max_val=T // H)
                with act.If(n_steps > 0):
                    with act.Fori(0, n_steps) as k:
                        s = act.snap(step, min_val=0, max_val=STEPS_MAX)
                        n = act.snap(full, min_val=0, max_val=STEPS_MAX)
                        sigmoid(0, s)
                        with act.If(2 * k + 1 >= n_halves):
                            take_xT(s + 1)
                            take_gT(0, s)
                        with act.If(2 * k + 1 < n_halves):
                            take_gT(0, s)
                            sigmoid(1, n)
                            take_xT(s + 1)
                            take_gT(1, n)
                            act.reg_add(full, full, 1)
                        act.reg_add(step, step, 1)
                act.nop()

            landed = act.alloc_register("act_landed")
            act.reg_mov(landed, 32)
            with act.Fori(0, E - 1) as e:
                expert(e)
                load = act.value_load(counts[0:1, 3, bass.ds(e + 1, 1)], min_val=0, max_val=16)
                with act.If(load > 0):
                    s = act.snap(step, min_val=0, max_val=STEPS_MAX)
                    value = act.snap(landed, min_val=32, max_val=32 * E)
                    for piece in range(2):
                        act.wait_ge(w2_used, 2 * s + (piece + 1))
                        apart(act)
                        act.wait_ge(w2_in[piece], value)
                        apart(act)
                        load_w2(act, e, piece, w2_v[1:E])
                    act.reg_add(landed, landed, 32)
                act.nop()
            expert(E - 1)

            for i in range(TT + 1):
                if i < TT:
                    act.wait_ge(y_in[i], 16)
                    nc.scalar.activation(fin[:, i, :], y_all[:, i, 0, :], ACT.Copy, scale=gates[:, i, 0:1])\
                        .then_inc(y_first, 1)
                if i == 0:
                    continue
                i -= 1
                act.wait_ge(f_sum, i + 1)
                nc.scalar.activation(fin_junk, fin[:, i, :], ACT.Square, accum_out=stat[:, 0, i:i + 1]).then_inc(f_sq, 1)
                act.wait_ge(f_sq, i + 1)
                root(stat[:, 1, i:i + 1])

        @block.vector
        def _(dve):
            link = linker(dve, dve_chain)
            TS, STT, TTo = nc.vector.tensor_scalar, nc.vector.scalar_tensor_tensor, nc.vector.tensor_tensor
            link(nc.vector.memset(xa_pad[:, :, 0:PADC], 0.0))

            rms_n = [0]

            def rstd(dst, src, link=link):
                rms_n[0] += 1
                TS(dst, src, 1.0 / D, EPS, ALU.mult, ALU.add).then_inc(ms_ok, 1)
                dve.wait_ge(rms_ok, rms_n[0])
                link(nc.vector.reciprocal(dst, dst))

            dve.wait_ge(vecT_ok, 1)
            nc.vector.tensor_copy(cols, bank[7][:, 0:48]).then_inc(cols_ok, 1)
            dve.wait_ge(cols_ok, 1)
            lam = cols[:, COL["lru_lambda"]:COL["lru_lambda"] + FT]
            STT(lru_c[:, 0, :], lam, -1.0, lam, ALU.mult, ALU.max).then_inc(lam_abs_ok, 1)
            dve.wait_ge(c_sig_ok, 1)
            link(TTo(c_sig, c_sig, c_col, ALU.mult))
            nc.vector.tensor_copy(c_rep, c_sig.unsqueeze(2).to_broadcast([P, KT, H])).then_inc(c_ok, 1)
            for i in range(TT):
                dve.wait_ge(x_sq, i + 1)
                rstd(stat[:, 1, i:i + 1], stat[:, 0, i:i + 1])
                TS(xn[:, i, :], x1[:, i, :], stat[:, 1, i:i + 1], None, ALU.mult).then_inc(xn_ok, 1)
            dve.wait_ge(lam_exp_ok, 1)
            z, q, q2, p = lru_c[:, 1, :], lru_c[:, 2, :], lru_c[:, 3, :], lru_c[:, 4, :]
            link(TS(q, z, 2.0, None, ALU.add))
            link(nc.vector.reciprocal(q, q))
            link(TTo(q, q, z, ALU.mult))
            link(TTo(q2, q, q, ALU.mult))
            link(TS(p, q2, 1.0 / 15, None, ALU.mult))
            for d in (13, 11, 9, 7, 5, 3):
                link(STT(p, p, 1.0 / d, q2, ALU.add, ALU.mult))
            link(STT(p, p, 1.0, q, ALU.add, ALU.mult))
            link(TS(q, lam, -1.0, 0.0, ALU.mult, ALU.max))
            link(STT(p, p, 2.0, q, ALU.mult, ALU.add))
            link(TS(lru_c[:, 5, :], p, -LRU_C, None, ALU.mult))
            link(TS(lru_c[:, 6, :], p, -2.0 * LRU_C, None, ALU.mult))
            TS(lru_c[:, 7, :], p, LRU_C, None, ALU.mult).then_inc(lru_c_ok, 1)
            link(TTo(pool_pb, cols[:, COL["pool_b"]:COL["pool_b"] + FT], cols[:, COL["pool_scale"]:COL["pool_scale"] + FT],
                     ALU.mult))
            dve.wait_ge(window_ok, 1)
            nc.vector.reciprocal(inv_count, inv_count).then_inc(pool_const, 1)

            def mod_vector(v):
                row = ada_rows[:, v, :]
                dve.wait_ge(ada_used, (v + 1) * (KT // AK))
                dve.wait_ge(rows_in, 5 * J * 16)
                add = TTo(row, bank[6 + v % 2][:, 0:QW], row, ALU.add)
                gain = {1: 0, 2: 1, 4: 2, 5: 3}.get(v)
                if gain is None:
                    add.then_inc(mod_row, 1)
                    return
                link(add)
                g = gain_rows[:, gain, :]
                if v in (1, 4):
                    STT(row, row, 1.0, g, ALU.add, ALU.mult).then_inc(mod_row, 1)
                else:
                    TTo(row, row, g, ALU.mult).then_inc(mod_row, 1)

            mod_vector(0)
            mod_vector(1)
            dve.wait_ge(mod_colT, 1)
            cT = bank[5][:, :].rearrange("p (v m j r) -> p v m j r", v=2, m=QM, j=J)
            for v in range(2):
                for m in range(QM):
                    last = nc.vector.tensor_copy(mod_col[:, v, :, m], cT[:, v, m, :, 0])
                    if (v, m) == (1, QM - 1):
                        last.then_inc(mod_col_ok, 1)
                    else:
                        link(last)
            for f in range(FT):
                dve.wait_ge(evac, number["xa", f] + 1)
                y = conv_x[:, f, :]
                for k in range(CONV):
                    w = cols[:, k * FT + f:k * FT + f + 1]
                    src = xa_pad[:, f % 2, PADC - k:PADC - k + T]
                    if k == 0:
                        link(TS(y, src, w, col("conv_b", f), ALU.mult, ALU.add))
                    elif k < CONV - 1:
                        link(STT(y, src, w, y, ALU.mult, ALU.add))
                    else:
                        STT(y, src, w, y, ALU.mult, ALU.add).then_inc(conv_ok, 1)
            dve.wait_ge(conv_ok, FT)

            def gelu_end(f):
                dve.wait_ge(gel_sig, f + 1)
                link(TTo(gel, gel, ga[:, f % 2, :], ALU.mult))
                TTo(catT[:, f, :], catT[:, f, :], gel, ALU.mult).then_inc(gel_ok, 1)

            for f in range(FT):
                mod_vector(2 + f)
                dve.wait_ge(lru_in, 3 * f + 3)
                th, b = tanh_m[:, f % 2, :], igate[:, f % 2, :]
                STT(th, decay2[:, f % 2, :], 1.0, th, ALU.add, ALU.mult).then_inc(m2_ok, 1)
                link(TTo(b, b, conv_x[:, f, :], ALU.mult))
                dve.wait_ge(root_ok, f + 1)
                link(TTo(b, b, th, ALU.mult))
                nc.vector.tensor_tensor_scan(catT[:, f, :], decay[:, f % 2, :], b, 0.0, ALU.mult, ALU.add)\
                    .then_inc(lru_ok, 1)
                dve.wait_ge(lru_ok, f + 1)
                if f:
                    gelu_end(f - 1)
                dve.wait_ge(evac, number["ga", f] + 1)
                g = ga[:, f % 2, :]
                if f:
                    dve.wait_ge(gel_ok, f)
                link(TTo(gel, g, g, ALU.mult))
                link(TS(gel, gel, 0.044715, 1.0, ALU.mult, ALU.add))
                TTo(gel, gel, g, ALU.mult).then_inc(gel_in, 1)
            gelu_end(FT - 1)

            for i in range(TT):
                dve.wait_ge(evac, number["mix", i, 1] + 1)
                link(TTo(stat[:, 4, i:i + 1], stat[:, 2, i:i + 1], stat[:, 3, i:i + 1], ALU.add))
                rstd(stat[:, 4, i:i + 1], stat[:, 4, i:i + 1])
                if i == 0:
                    dve.wait_ge(bc_ok, 8)
                m = mixb[:, i % 2, :]
                link(STT(m, m, stat[:, 4, i:i + 1], bc[:, 0, :], ALU.mult, ALU.mult))
                TTo(x1[:, i, :], x1[:, i, :], m, ALU.add).then_inc(x1_ok, 1)
                dve.wait_ge(x1_ok, i + 1)
                dve.wait_ge(x1_sq, i + 1)
                rstd(stat[:, 6, i:i + 1], stat[:, 5, i:i + 1])
                if i >= 2:
                    dve.wait_ge(evac, number["hT", i - 2, 1] + 1)
                    dve.wait_ge(h_stored[i % 2], 16 * (i // 2))
                h = hn[:, i % 2, :]
                link(STT(h, x1[:, i, :], stat[:, 6, i:i + 1], bc[:, 2, :], ALU.mult, ALU.mult))
                TTo(h, h, bc[:, 1, :], ALU.add).then_inc(hn_ok, 1)

            dve.wait_ge(evac, number["logits", TT - 1] + 1)
            dve.wait_ge(router_in, 32)
            dve.wait_ge(route_const, 5)
            dve.wait_ge(hn_ok, TT)

            def over(v, axis, *shape):
                return v.unsqueeze(axis).to_broadcast(list(shape))
            for j in range(J):
                link(nc.vector.memset(j_off[H * j:H * j + H, 0:1], float(j)))
                link(nc.vector.memset(j_off[H * j:H * j + H, 1:2], float(j - N2)))
            link(TTo(logits, logits, over(router_bias[:, :], 1, P, TT, E), ALU.add))
            for i in range(TT):
                link(nc.vector.max(top[:, i, :], logits[:, i, :]))
                link(nc.vector.max_index(top_i[:, i, :], top[:, i, :], logits[:, i, :]))
            link(nc.vector.tensor_copy(tk_f[:, 0, :].rearrange("p (i k) -> p i k", i=TT), top_i[:, :, 0:TOPK]))
            link(TTo(hot_e.rearrange("p i k e -> p (i k) e"), over(iota_e, 1, P, TK, E), over(tk_f[:, 0, :], 2, P, TK, E),
                     ALU.is_equal))
            link(TTo(sel, hot_e[:, :, 0, :], hot_e[:, :, 1, :], ALU.add))
            link(TTo(sel, sel, hot_e[:, :, 2, :], ALU.add))
            TTo(sel, sel, hot_e[:, :, 3, :], ALU.add).then_inc(sel_ok, 1)
            TTo(top_d, top[:, :, 0:TOPK], top[:, :, 0:1].to_broadcast([P, TT, TOPK]), ALU.subtract).then_inc(top_ok, 1)
            dve.wait_ge(top_exp, 1)
            link(nc.vector.reduce_sum(top_d[:, :, 0], top_e, axis=AX.X))
            link(nc.vector.reciprocal(top_d[:, :, 1], top_d[:, :, 0]))
            link(TTo(gates[:, :, :], top_e, top_d[:, :, 1:2].to_broadcast([P, TT, TOPK]), ALU.mult))
            dve.wait_ge(rank_ok, 1)
            link(TS(exp_i[:, 0, :], bank[5][:, 0:E], float(H - 1), None, ALU.add))
            link(TS(exp_i[:, 1, :], exp_i[:, 0, :], 5, None, ALU.arith_shift_right))
            link(TS(exp_i[:, 0, :], exp_i[:, 1, :], 1, None, ALU.add))
            link(TS(exp_i[:, 2, :], exp_i[:, 0, :], 1, None, ALU.arith_shift_right))
            link(TS(exp_i[:, 0, :], exp_i[:, 1, :], 1, None, ALU.arith_shift_right))
            nc.vector.tensor_copy(counts[0:1, 0, :], exp_i[0:1, 2, :]).then_inc(counts_ok, 1)
            nc.vector.tensor_copy(counts[0:1, 1, :], exp_i[0:1, 1, :]).then_inc(counts_ok, 1)
            nc.vector.tensor_copy(counts[0:1, 2, :], exp_i[0:1, 0, :]).then_inc(counts_ok, 1)
            link(TS(exp_f[:, 0, :], exp_i[:, 2, :], 1.0, 16.0, ALU.min, ALU.mult))
            link(nc.vector.memset(exp_f[:, 0, 0:1], 16.0))
            link(nc.vector.tensor_copy(counts[0:1, 3, :], exp_f[0:1, 0, :]))
            dve.sem_inc(counts_ok, 1)
            link(nc.vector.tensor_copy(exp_f[:, 0, :], exp_i[:, 2, :]))
            link(nc.vector.tensor_tensor_scan(exp_f[:, 1, :], ones[:, 0:E], exp_f[:, 0, :], 0.0, ALU.mult, ALU.add))
            link(TTo(exp_f[:, 2, :], exp_f[:, 1, :], exp_f[:, 0, :], ALU.subtract))
            link(TS(exp_f[:, 3, :], exp_f[:, 2, :], float(2 * H), None, ALU.mult))
            link(TTo(slot_e, bank[4][:, 0:TT * E].rearrange("p (i e) -> p i e", i=TT), over(exp_f[:, 3, :], 1, P, TT, E),
                     ALU.add))
            link(TTo(route_tmp.rearrange("p (i k) e -> p i k e", i=TT), hot_e, over(slot_e, 2, P, TT, TOPK, E), ALU.mult))
            link(nc.vector.reduce_sum(tk_f[:, 1, :], route_tmp, axis=AX.X))
            link(nc.vector.tensor_copy(tk_i[:, 0, :], tk_f[:, 1, :]))
            link(TS(tk_i[:, 1, :], tk_i[:, 0, :], 5, None, ALU.arith_shift_right))
            link(TS(tk_i[:, 2, :], tk_i[:, 0, :], H - 1, None, ALU.bitwise_and))
            link(nc.vector.tensor_copy(tk_f[:, 2:4, :], tk_i[:, 1:3, :]))
            link(TTo(hot_t, over(iota_t, 1, P, TK, P), over(tk_f[:, 3, :], 2, P, TK, P), ALU.is_equal))
            link(TTo(slot_val, over(iota_q, 1, P, TK, NQ), over(tk_f[:, 2, :], 2, P, TK, NQ), ALU.is_equal))
            TTo(slot_val, slot_val, over(tok_no, 2, P, TK, NQ), ALU.mult).then_inc(slots_ok, 1)
            dve.wait_ge(table_ok, 1)
            tab = bank[6][:, 0:NQ]
            link(TS(idx_n, tab, -1.0, None, ALU.add))
            link(TS(idx_e, tab, 0.0, float(EMPTY), ALU.is_equal, ALU.mult))
            link(TS(idx_n, idx_n, -TOPK, None, ALU.bitwise_and))
            link(TS(idx_f[:, 1, :], tab, float(N2), j_off[:, 1:2], ALU.mult, ALU.add))
            link(TS(idx_f[:, 0, :], idx_n, j_off[:, 0:1], None, ALU.add))
            TTo(idx.rearrange("p v s h -> p v (s h)"), idx_f, over(idx_e, 1, P, 2, NQ), ALU.add).then_inc(idx_ok, 1)
            dve.wait_ge(idx_ok, 1)

            def activate(hf, n, slot, bias_arrived):
                dve.wait_ge(bias_in[slot], bias_arrived)
                dve.wait_ge(u_ps[hf], n + 1)
                gate, lin = u_parts(hf)[:, :, 0], u_parts(hf)[:, :, 1]
                TTo(u_sb[:, hf, :], bank[hf][:, :], b1_bc[:, slot, :], ALU.add).then_inc(u_ok[hf], 1)
                dve.wait_ge(u_ok[hf], n + 1)
                TS(gate, gate, LIMIT, None, ALU.min).then_inc(glu_ok[hf], 1)
                TS(lin, lin, LIMIT, -LIMIT, ALU.min, ALU.max).then_inc(lin_ok[hf], 1)
                dve.wait_ge(lin_ok[hf], n + 1)
                STT(lin, lin, 1.0, gate, ALU.add, ALU.mult).then_inc(mul_ok[hf], 1)
                dve.wait_ge(mul_ok[hf], n + 1)
                dve.wait_ge(sig_ok[hf], n + 1)
                TTo(act_g[:, hf, :], lin, act_g[:, hf, :], ALU.mult).then_inc(act_ok[hf], 1)

            def finish(hf, n, slot):
                dve.wait_ge(y_ps[hf], n + 1)
                TTo(y_part[:, hf, :], bank[4 + hf][YP:2 * YP, :], b2_bc[:, slot, :], ALU.add).then_inc(y_part_ok[hf], 1)
                dve.wait_ge(y_part_ok[hf], n + 1)
                dve.wait_ge(y_stored[hf], 16 * n + 16)
                TTo(y_sb[hf], bank[4 + hf][0:YP, :], y_part[:, hf, :], ALU.add).then_inc(y_ok[hf], 1)

            dve.wait_ge(counts_ok, 4)
            step, full = dve.alloc_register("dve_step"), dve.alloc_register("dve_full")
            dve.reg_mov(step, 0)
            dve.reg_mov(full, 0)
            landed = [dve.alloc_register(f"dve_landed{v}") for v in range(2)]
            dve.reg_mov(landed[0], 0)
            dve.reg_mov(landed[1], 16)
            with dve.Fori(0, E // 2) as pair:
                for slot in range(2):
                    e = 2 * pair + slot
                    n_steps = dve.value_load(counts[0:1, 0, bass.ds(e, 1)], min_val=0, max_val=T // (2 * H))
                    n_halves = dve.value_load(counts[0:1, 1, bass.ds(e, 1)], min_val=0, max_val=T // H)
                    load = dve.value_load(counts[0:1, 3, bass.ds(e, 1)], min_val=0, max_val=16)
                    dve.reg_add(landed[slot], landed[slot], load)
                    bias_arrived = (J + N2) * dve.snap(landed[slot], min_val=16, max_val=16 * E)
                    with dve.If(n_steps > 0):
                        with dve.Fori(0, n_steps) as k:
                            s = dve.snap(step, min_val=0, max_val=STEPS_MAX)
                            n = dve.snap(full, min_val=0, max_val=STEPS_MAX)
                            activate(0, s, slot, bias_arrived)
                            with dve.If(2 * k + 1 < n_halves):
                                activate(1, n, slot, bias_arrived)
                            finish(0, s, slot)
                            with dve.If(2 * k + 1 < n_halves):
                                finish(1, n, slot)
                                dve.reg_add(full, full, 1)
                            dve.reg_add(step, step, 1)
                dve.nop()

            link2 = linker(dve, f_chain)
            for i in range(TT + 1):
                if i < TT:
                    dve.wait_ge(y_first, i + 1)
                    dve.wait_ge(y_in[i], 16)
                    f = fin[:, i, :]
                    for k in range(1, TOPK):
                        ins = STT(f, y_all[:, i, k, :], gates[:, i, k:k + 1], f, ALU.mult, ALU.add)
                        if k < TOPK - 1:
                            link2(ins)
                        else:
                            ins.then_inc(f_sum, 1)
                if i >= 1:
                    dve.wait_ge(f_sq, i)
                    rstd(stat[:, 1, i - 1:i], stat[:, 0, i - 1:i], link2)
                    f = fin[:, i - 1, :]
                    STT(f, f, stat[:, 1, i - 1:i], gate_f_bc[:, :], ALU.mult, ALU.mult).then_inc(f_scaled, 1)

        @block.tensor
        def _(pe):
            mm, tr = nc.tensor.matmul, nc.tensor.transpose
            pe.wait_ge(ident_ok, 2)
            pe.wait_ge(vec_in, 8 * 16)
            tr(bank[7][:, 0:48], vec_rows[0:48, :], ident[0:48, 0:48]).then_inc(vecT_ok, 1)

            def ready(what):
                n = number[what]
                if n >= R:
                    pe.wait_ge(evac, n - R + 1)
                return bank[n % R]

            def mod(v):
                if v == 1:
                    pe.wait_ge(cols_ok, 1)
                if v >= 2:
                    pe.wait_ge(mod_row, v - 1)
                for kk in range(KT // AK):
                    n = v * (KT // AK) + kk
                    pe.wait_ge(ada_in[n % ADA_RING], 16 * (n // ADA_RING + 1))
                    for k in range(AK):
                        for j in range(J):
                            last = mm(bank[6 + v % 2][H * j:H * j + H, 0:QW], c_rep[:, kk * AK + k, :],
                                      ada_ring[:, n % ADA_RING, k, QW * j:QW * j + QW],
                                      start=(kk == 0 and k == 0), stop=(kk == KT // AK - 1 and k == AK - 1))
                    last.then_inc(ada_used, 1)

            pe.wait_ge(c_ok, 1)
            mod(0)
            pe.wait_ge(xn_ok, TT)
            for k in range(R):
                ps = ready(("xT", k))
                for i in range(TT):
                    last = tr(ps[:, i * P:(i + 1) * P], xn[:, i, k * P:(k + 1) * P], ident[:, :])
                last.then_inc(prod, 1)
            mod(1)
            pe.wait_ge(mod_row, 2)
            for v in range(2):
                for m in range(QM):
                    at = (v * QM + m) * P
                    last = tr(bank[5][:, at:at + P], ada_rows[:, v, m * P:(m + 1) * P], ident[:, :])
            last.then_inc(mod_colT, 1)
            for k in range(R, KT):
                ps = ready(("xT", k))
                for i in range(TT):
                    last = tr(ps[:, i * P:(i + 1) * P], xn[:, i, k * P:(k + 1) * P], ident[:, :])
                last.then_inc(prod, 1)
            pe.wait_ge(evac, KT)

            def u_part(name, slot, count):
                pe.wait_ge(win_in[slot], 16 * count)
                for f in range(FT):
                    ps = ready((name, f))
                    for k in range(KT):
                        last = mm(ps[:, :], win_ring[:, slot, k, f * P:(f + 1) * P], hT[:, k, :], start=(k == 0),
                                  stop=(k == KT - 1))
                    last.then_inc(prod, 1)
                    yield f

            for _ in u_part("xa", 0, 1):
                pass
            for _ in u_part("xb", 1, 1):
                pass
            pe.wait_ge(bd_in, 4 * 16)
            ga_parts = u_part("ga", 0, 2)
            for f in range(FT):
                mod(2 + f)
                pe.wait_ge(conv_ok, f + 1)
                for n, name in enumerate(("r", "i")):
                    ps = ready((name, f))
                    mm(ps[:, :], gate_bd[:, n, f, :], conv_x[:, f, :], start=True, stop=True).then_inc(prod, 1)
                next(ga_parts)
            pe.wait_ge(pool_in, 16)
            for g in range(FT):
                pe.wait_ge(pool_ok, g + 1)
                ps = ready(("pool", g))
                mm(ps[:, :], pool_sb[:, g, :], catT[:, FT + g, :], start=True, stop=True).then_inc(prod, 1)
            pe.wait_ge(mod_row, 6)
            for v in range(4):
                if v >= 2:
                    pe.wait_ge(bc_ok, 2 * v - 2)
                for j in range(J):
                    last = mm(bank[4 + 2 * (v % 2) + j // 2][:, (j % 2) * QW:(j % 2 + 1) * QW],
                              ident[:, H * j:H * j + 1].to_broadcast([P, P]), ada_rows[:, 2 + v, :], start=True, stop=True)
                last.then_inc(bc_ps, 1)
            pe.wait_ge(wout_in, 16)
            pe.wait_ge(gel_ok, FT)
            pe.wait_ge(evac, number["pool", FT - 1] + 1)
            pe.wait_ge(router_in, 32)
            for what in order[number["mix", 0, 0]:]:
                i = what[1]
                if what[0] == "hT":
                    pe.wait_ge(hn_ok, i + 1)
                if what[0] == "logits":
                    pe.wait_ge(evac, number["hT", i, 1] + 1)
                ps = ready(what)
                if what[0] == "mix":
                    n = what[2]
                    for k in range(KT):
                        last = mm(ps[:, :], catT[:, k, i * P:(i + 1) * P], W2[:, k, n * 512:(n + 1) * 512],
                                  start=(k == 0), stop=(k == KT - 1))
                elif what[0] == "hT":
                    for k in range(HALF):
                        col_at = (what[2] * HALF + k) * P
                        last = tr(ps[:, k * P:(k + 1) * P], hn[:, i % 2, col_at:col_at + P], ident[:, :])
                else:
                    for k in range(KT):
                        last = mm(ps[:, 0:E], h2T[:, i % 2, k, :], router_sb[:, k, :], start=(k == 0), stop=(k == KT - 1))
                last.then_inc(prod, 1)

            pe.wait_ge(route_const, 5)
            pe.wait_ge(sel_ok, 1)
            pe.wait_ge(bc_ok, 8)
            for i in range(TT):
                for b in range(i + 1):
                    mm(bank[4][:, i * E:(i + 1) * E], upper if b == i else ones[:, :], sel[:, b, :], start=(b == 0),
                       stop=(b == i))
            for i in range(TT):
                last = mm(bank[5][:, 0:E], ones[:, :], sel[:, i, :], start=(i == 0), stop=(i == TT - 1))
            last.then_inc(rank_ok, 1)
            pe.wait_ge(slots_ok, 1)
            for n in range(TK):
                last = mm(bank[6][:, 0:NQ], hot_t[:, n, :], slot_val[:, n, :], start=(n == 0), stop=(n == TK - 1))
            last.then_inc(table_ok, 1)

            def transpose_x(s, first=False):
                pe.wait_ge(xg_in, 32 * s + 32)
                if not first:
                    pe.wait_ge(xT_ok, s)
                for hf in range(2):
                    for m in range(QM):
                        at = (hf * QM + m) * P
                        last = tr(bank[2][:, at:at + P], xg[hf][:, m * P:(m + 1) * P], ident[:, :])
                last.then_inc(xT_ps, 1)

            def up(halves, slot, arrived):
                lag = LAG if len(halves) == 2 else 0
                for at in range(KT + lag):
                    for hf in halves:
                        k = at - lag * hf
                        if not 0 <= k < KT:
                            continue
                        if hf == 0:
                            pe.wait_ge(w1_in[slot][k], arrived)
                        for j in range(J):
                            last = mm(bank[hf][H * j:H * j + H, :], xT[:, hf, k % QM, H * (k // QM):H * (k // QM) + H],
                                      W1[:, slot, k, UW * j:UW * j + UW], start=(k == 0), stop=(k == KT - 1))
                        if k == KT - 1:
                            last.then_inc(u_ps[hf], 1)
                        elif hf == halves[-1]:
                            last.then_inc(w1_used, 1)
                pe.drain().then_inc(w1_used, 1)

            def transpose_g(hf, n):
                pe.wait_ge(act_ok[hf], n + 1)
                for m in range(QM):
                    last = tr(gT_bank[hf][:, m * P:(m + 1) * P], act_g[:, hf, m * P:(m + 1) * P], ident[:, :])
                last.then_inc(gT_ps[hf], 1)

            def down(hf, n, arrived, *tiles, left=False):
                for kk in tiles:
                    if kk == 0:
                        pe.wait_ge(gT_ok[hf], n + 1)
                    if kk % 2 == 0:
                        pe.wait_ge(w2_in[kk // 2], arrived)
                    for a in range(2):
                        k = a * HALF + kk
                        for piece in range(N2):
                            j = N2 * a + piece
                            last = mm(bank[4 + hf][H * j:H * j + H, :], gT[:, hf, k % QM, H * (k // QM):H * (k // QM) + H],
                                      W2[:, k, HW * piece:HW * piece + HW], start=(kk == 0), stop=(kk == HALF - 1))
                    if kk == HALF - 1:
                        last.then_inc(y_ps[hf], 1)
                    elif left and kk == 1:
                        last.then_inc(w2_used, 1)

            LAG = 3
            pe.sem_inc(w1_used, KT)
            pe.sem_inc(w2_used, 2)
            transpose_x(0, first=True)
            pe.wait_ge(counts_ok, 4)
            step, full = pe.alloc_register("pe_step"), pe.alloc_register("pe_full")
            pe.reg_mov(step, 0)
            pe.reg_mov(full, 0)
            landed = [pe.alloc_register(f"pe_landed{v}") for v in range(3)]
            for v in range(3):
                pe.reg_mov(landed[v], 16 if v == 1 else 0)
            halves = pe.alloc_register("pe_halves")
            counts_row = counts[:, 1:3, :].rearrange("p a e -> p (a e)")

            def load_halves(e):
                pe.reg_mov(halves, pe.value_load(counts_row[0:1, bass.ds(e, 1)], min_val=0, max_val=T // H))

            load_halves(0)
            first_halves = pe.snap(halves, min_val=0, max_val=T // H)
            with pe.If(first_halves < 1):
                pe.reg_add(landed[0], landed[0], 16)
                pe.reg_add(landed[2], landed[2], 32)
            with pe.Fori(0, E // 2) as pair:
                for slot in range(2):
                    e = 2 * pair + slot
                    n_halves = pe.snap(halves, min_val=0, max_val=T // H)
                    with pe.If(n_halves > 0):
                        pe.reg_add(landed[slot], landed[slot], 16)
                        pe.reg_add(landed[2], landed[2], 32)
                        w1_arrived = pe.snap(landed[slot], min_val=16, max_val=16 * E)
                        w2_arrived = pe.snap(landed[2], min_val=32, max_val=32 * E)
                        n_full = n_halves >> 1
                        with pe.If(n_full > 0):
                            with pe.Fori(0, n_full):
                                s = pe.snap(step, min_val=0, max_val=STEPS_MAX)
                                n = pe.snap(full, min_val=0, max_val=STEPS_MAX)
                                pe.wait_ge(xT_ok, s + 1)
                                up((0, 1), slot, w1_arrived)
                                transpose_g(0, s)
                                transpose_x(s + 1)
                                down(0, s, w2_arrived, 0, 1)
                                transpose_g(1, n)
                                down(0, s, w2_arrived, 2)
                                down(1, n, w2_arrived, 0, 1, left=True)
                                down(0, s, w2_arrived, 3)
                                down(1, n, w2_arrived, 2, 3)
                                pe.drain().then_inc(w2_used, 1)
                                pe.reg_add(full, full, 1)
                                pe.reg_add(step, step, 1)
                        with pe.If((n_halves & 1) > 0):
                            s = pe.snap(step, min_val=0, max_val=STEPS_MAX)
                            pe.wait_ge(xT_ok, s + 1)
                            up((0,), slot, w1_arrived)
                            transpose_x(s + 1)
                            load_halves(e + 1)
                            transpose_g(0, s)
                            down(0, s, w2_arrived, 0, 1, 2, 3, left=True)
                            pe.drain().then_inc(w2_used, 1)
                            pe.reg_add(step, step, 1)
                    with pe.If((n_halves & 1) < 1):
                        load_halves(e + 1)
                pe.nop()
    return nc


_INS = ["x", "c", "w_ada", "b_ada", "norm_mix_pre", "norm_mix_post", "w_in", "conv_w", "conv_b", "gate_a_w", "gate_a_b",
        "gate_x_w", "gate_x_b", "lru_lambda", "pool_w", "pool_b", "pool_scale", "w_out", "norm_ffn_pre",
        "norm_ffn_post", "router_w", "router_b", "expert_w1", "expert_b1", "expert_w2", "expert_b2"]


def kernel(**inputs):
    import numpy as _np
    import concourse.bacc as _bacc
    from concourse import mybir as _mybir
    from concourse.bass_utils import run_bass_kernel_spmd as _run

    nc = _bacc.Bacc("TRN2", target_bir_lowering=False, num_devices=1)
    arrays, args = {}, []
    for name in _INS:
        a = _np.ascontiguousarray(inputs[name])
        arrays[f"in_{name}"] = a
        args.append(nc.dram_tensor(f"in_{name}", a.shape, _mybir.dt.from_np(a.dtype), kind="ExternalInput").ap())
    out = nc.dram_tensor("out_0", arrays["in_x"].shape, _mybir.dt.float32, kind="ExternalOutput").ap()
    hybrid_layer(nc, *args, out)
    r = _run(nc, [arrays], core_ids=[0])
    return r.results[0]["out_0"]
```
